# Optimizing a Trainium2 kernel written in Bass

```python
import jax, jax.numpy as jnp
from jax import lax
import numpy as np

D_MODEL = 1024
BATCH = 1
SEQ = 1024
DEPTH = 1
DEC_BATCH = 1
DEC_SEQ = 1024
PAST_LEN = 128

GRID_W = 64
MIX_WIDTH = D_MODEL
MLSTM_WIDTH = MIX_WIDTH // 2
MLSTM_HEADS = 4
MLSTM_HEAD_DIM = MLSTM_WIDTH // MLSTM_HEADS
MLSTM_CHUNK = 128
NA_WIDTH = MIX_WIDTH - MLSTM_WIDTH
NA_HEAD_DIM = 64
NA_HEADS = NA_WIDTH // NA_HEAD_DIM
NA_MAX_KH = 8
NA_KW = 16
N_GATE_COLS = 2 * 2 * MLSTM_HEADS
IN_SPLITS = (MLSTM_WIDTH, MLSTM_WIDTH, MLSTM_WIDTH, MLSTM_WIDTH, N_GATE_COLS, NA_WIDTH, NA_WIDTH, NA_WIDTH)
IN_COLS = sum(IN_SPLITS)
IN_SPLIT_POINTS = tuple(int(s) for s in np.cumsum(IN_SPLITS)[:-1])
N_EXPERTS = 16
EC_CAPACITY_FACTOR = 2
D_EXPERT = D_MODEL
N_MOD = 6
RMS_EPS = 1e-6

kernel_name = "hymba_mlstm_natten_ec_encoder"

def rmsnorm(x, g):
    xf = x.astype(jnp.float32)
    y = xf * lax.rsqrt(jnp.mean(xf * xf, axis=-1, keepdims=True) + RMS_EPS)
    return (y * g.astype(jnp.float32)).astype(x.dtype)

def mlstm_chunkwise(q, k, v, log_i, log_f):
    B, H, T, d = q.shape
    L = MLSTM_CHUNK
    nc = T // L
    q = q.astype(jnp.float32).reshape(B, H, nc, L, d)
    k = (k.astype(jnp.float32) * (d ** -0.5)).reshape(B, H, nc, L, d)
    v = v.astype(jnp.float32).reshape(B, H, nc, L, d)
    li = log_i.astype(jnp.float32).reshape(B, H, nc, L)
    lf = log_f.astype(jnp.float32).reshape(B, H, nc, L)
    b = jnp.cumsum(lf, axis=-1)
    g = b[..., -1]
    a = g[..., None] - b + li
    m_loc = jnp.max(a, axis=-1)
    w = jnp.exp(a - m_loc[..., None])
    C_loc = jnp.einsum('bhcs,bhcsv,bhcsk->bhcvk', w, v, k)
    n_loc = jnp.einsum('bhcs,bhcsk->bhck', w, k)

    def step(carry, inp):
        C, n, m = carry
        g_c, m_l, C_l, n_l = inp
        m_new = jnp.maximum(g_c + m, m_l)
        s_old = jnp.exp(g_c + m - m_new)
        s_loc = jnp.exp(m_l - m_new)
        C_new = s_old[..., None, None] * C + s_loc[..., None, None] * C_l
        n_new = s_old[..., None] * n + s_loc[..., None] * n_l
        return (C_new, n_new, m_new), (C, n, m)

    init = (jnp.zeros((B, H, d, d), jnp.float32), jnp.zeros((B, H, d), jnp.float32), jnp.zeros((B, H), jnp.float32))
    xs = (jnp.moveaxis(g, 2, 0), jnp.moveaxis(m_loc, 2, 0), jnp.moveaxis(C_loc, 2, 0), jnp.moveaxis(n_loc, 2, 0))
    _, (C_s, n_s, m_s) = lax.scan(step, init, xs)
    C_s = jnp.moveaxis(C_s, 0, 2)
    n_s = jnp.moveaxis(n_s, 0, 2)
    m_s = jnp.moveaxis(m_s, 0, 2)

    tril = np.tril(np.ones((L, L), dtype=bool))
    Dlog = jnp.where(tril, b[..., :, None] - b[..., None, :] + li[..., None, :], -jnp.inf)
    inter = b + m_s[..., None]
    m_out = jnp.maximum(jnp.max(Dlog, axis=-1), inter)
    S = jnp.einsum('bhcjd,bhcsd->bhcjs', q, k) * jnp.exp(Dlog - m_out[..., None])
    s_int = jnp.exp(inter - m_out)
    num = jnp.einsum('bhcjs,bhcsv->bhcjv', S, v) + s_int[..., None] * jnp.einsum('bhcvk,bhcjk->bhcjv', C_s, q)
    den = jnp.sum(S, axis=-1) + s_int * jnp.einsum('bhck,bhcjk->bhcj', n_s, q)
    h = num / jnp.maximum(jnp.abs(den), jnp.exp(-m_out))[..., None]
    return h.reshape(B, H, T, d)

def neighbourhood_attention(q, k, v, rel_bias):
    B, T, H, d = q.shape
    rows = T // GRID_W
    kh = min(NA_MAX_KH, rows)
    qg = q.reshape(B, rows, GRID_W, H, d)
    kg = k.reshape(B, rows, GRID_W, H, d)
    vg = v.reshape(B, rows, GRID_W, H, d)
    cols = np.arange(GRID_W)
    col_start = np.clip(cols - NA_KW // 2, 0, GRID_W - NA_KW)
    col_idx = col_start[:, None] + np.arange(NA_KW)[None, :]
    dc_idx = col_idx - cols[:, None] + (NA_KW - 1)
    bias_c = rel_bias[:, :, dc_idx]
    scale = d ** -0.5

    def row_fn(r):
        r0 = jnp.clip(r - kh // 2, 0, rows - kh)
        k_rows = lax.dynamic_slice_in_dim(kg, r0, kh, axis=1)
        v_rows = lax.dynamic_slice_in_dim(vg, r0, kh, axis=1)
        k_win = k_rows[:, :, col_idx]
        v_win = v_rows[:, :, col_idx]
        q_r = lax.dynamic_index_in_dim(qg, r, axis=1, keepdims=False)
        s = jnp.einsum('bchd,bicjhd->bhcij', q_r, k_win).astype(jnp.float32) * scale
        dr_idx = r0 + jnp.arange(kh) - r + (NA_MAX_KH - 1)
        bias = jnp.take(bias_c, dr_idx, axis=1).transpose(0, 2, 1, 3)
        s = s + bias[None].astype(jnp.float32)
        p = jax.nn.softmax(s.reshape(B, H, GRID_W, kh * NA_KW), axis=-1).reshape(B, H, GRID_W, kh, NA_KW)
        return jnp.einsum('bhcij,bicjhd->bchd', p.astype(v.dtype), v_win)

    out = lax.map(row_fn, jnp.arange(rows))
    return out.transpose(1, 0, 2, 3, 4).reshape(B, T, H * d)

def token_mixer(h, w_in, b_gates, g_mlstm, na_rel_bias, w_out):
    B, T, _ = h.shape
    proj = h @ w_in
    q_m, k_m, v_m, o_m, gates, q_n, k_n, v_n = jnp.split(proj, IN_SPLIT_POINTS, axis=-1)
    to_heads = lambda t: t.reshape(B, T, MLSTM_HEADS, MLSTM_HEAD_DIM).transpose(0, 2, 1, 3)
    q_m, k_m, v_m = to_heads(q_m), to_heads(k_m), to_heads(v_m)
    gt = gates.astype(jnp.float32).reshape(B, T, 2, 2, MLSTM_HEADS) + b_gates.astype(jnp.float32)
    gt = jnp.transpose(gt, (2, 3, 0, 4, 1))
    h_fwd = mlstm_chunkwise(q_m, k_m, v_m, gt[0, 0], jax.nn.log_sigmoid(gt[0, 1]))
    flip = lambda t: jnp.flip(t, axis=2)
    h_bwd = flip(mlstm_chunkwise(flip(q_m), flip(k_m), flip(v_m), jnp.flip(gt[1, 0], axis=-1),
                                 jnp.flip(jax.nn.log_sigmoid(gt[1, 1]), axis=-1)))
    hm = (h_fwd + h_bwd).transpose(0, 2, 1, 3)
    hm = hm * lax.rsqrt(jnp.mean(hm * hm, axis=-1, keepdims=True) + RMS_EPS) * g_mlstm.astype(jnp.float32)
    hm = (hm.reshape(B, T, MLSTM_WIDTH) * jax.nn.sigmoid(o_m.astype(jnp.float32))).astype(h.dtype)
    to_na = lambda t: t.reshape(B, T, NA_HEADS, NA_HEAD_DIM)
    hn = neighbourhood_attention(to_na(q_n), to_na(k_n), to_na(v_n), na_rel_bias)
    return jnp.concatenate([hm, hn.astype(h.dtype)], axis=-1) @ w_out

def expert_choice_moe(h, w_router, w_gate, w_up, w_down):
    B, T, D = h.shape
    n = B * T
    xf = h.reshape(n, D)
    aff = jax.nn.softmax((xf @ w_router).astype(jnp.float32), axis=-1)
    cap = EC_CAPACITY_FACTOR * n // N_EXPERTS
    gate, idx = lax.top_k(aff.T, cap)
    xe = xf[idx]
    hid = jax.nn.silu(jnp.einsum('ecd,edf->ecf', xe, w_gate)) * jnp.einsum('ecd,edf->ecf', xe, w_up)
    ye = jnp.einsum('ecf,efd->ecd', hid, w_down) * gate[..., None].astype(h.dtype)
    y = jnp.zeros_like(xf).at[idx.reshape(-1)].add(ye.reshape(-1, D))
    return y.reshape(B, T, D)

def encoder_layer(x, c, w_ada, b_ada, g_pre_mix, g_post_mix, w_in, b_gates, g_mlstm, na_rel_bias, w_out,
                  g_pre_ffn, g_post_ffn, w_router, w_expert_gate, w_expert_up, w_expert_down):
    B = x.shape[0]
    mod = (jax.nn.silu(c) @ w_ada + b_ada).reshape(B, N_MOD, D_MODEL)[:, :, None, :]
    shift1, scale1, gate1, shift2, scale2, gate2 = [mod[:, i] for i in range(N_MOD)]
    h = rmsnorm(x, g_pre_mix) * (1 + scale1) + shift1
    x = x + gate1 * rmsnorm(token_mixer(h, w_in, b_gates, g_mlstm, na_rel_bias, w_out), g_post_mix)
    h = rmsnorm(x, g_pre_ffn) * (1 + scale2) + shift2
    x = x + gate2 * rmsnorm(expert_choice_moe(h, w_router, w_expert_gate, w_expert_up, w_expert_down), g_post_ffn)
    return x

def trunk(x, c, w_ada, b_ada, g_pre_mix, g_post_mix, w_in, b_gates, g_mlstm, na_rel_bias, w_out,
          g_pre_ffn, g_post_ffn, w_router, w_expert_gate, w_expert_up, w_expert_down):
    for l in range(DEPTH):
        x = encoder_layer(x, c, w_ada[l], b_ada[l], g_pre_mix[l], g_post_mix[l], w_in[l], b_gates[l], g_mlstm[l],
                          na_rel_bias[l], w_out[l], g_pre_ffn[l], g_post_ffn[l], w_router[l],
                          w_expert_gate[l], w_expert_up[l], w_expert_down[l])
    return x

def setup_inputs(seed: int = 0) -> dict:
    key = jax.random.key(seed)
    ks = jax.random.split(key, 24)
    nrm = lambda k, shape, s: jax.random.normal(k, shape, jnp.float32) * s
    gain = lambda k, shape: 1.0 + 0.05 * jax.random.normal(k, shape, jnp.float32)
    b_i = nrm(ks[10], (DEPTH, 2, MLSTM_HEADS), 0.1)
    b_f = jnp.linspace(3.0, 6.0, MLSTM_HEADS) + nrm(ks[11], (DEPTH, 2, MLSTM_HEADS), 0.1)
    return {
        'x_prompt': nrm(ks[0], (BATCH, SEQ, D_MODEL), 1.0),
        'x_sample': nrm(ks[1], (DEC_BATCH, DEC_SEQ, D_MODEL), 1.0),
        'c_prompt': nrm(ks[2], (BATCH, D_MODEL), 1.0),
        'c_sample': nrm(ks[3], (DEC_BATCH, D_MODEL), 1.0),
        'w_ada': nrm(ks[4], (DEPTH, D_MODEL, N_MOD * D_MODEL), 0.5 * D_MODEL ** -0.5),
        'b_ada': nrm(ks[5], (DEPTH, N_MOD * D_MODEL), 0.01),
        'g_pre_mix': gain(ks[6], (DEPTH, D_MODEL)),
        'g_post_mix': gain(ks[7], (DEPTH, D_MODEL)),
        'w_in': nrm(ks[8], (DEPTH, D_MODEL, IN_COLS), D_MODEL ** -0.5),
        'b_gates': jnp.stack([b_i, b_f], axis=2),
        'g_mlstm': gain(ks[12], (DEPTH, MLSTM_HEADS, MLSTM_HEAD_DIM)),
        'na_rel_bias': nrm(ks[13], (DEPTH, NA_HEADS, 2 * NA_MAX_KH - 1, 2 * NA_KW - 1), 0.1),
        'w_out': nrm(ks[14], (DEPTH, MIX_WIDTH, D_MODEL), MIX_WIDTH ** -0.5),
        'g_pre_ffn': gain(ks[15], (DEPTH, D_MODEL)),
        'g_post_ffn': gain(ks[16], (DEPTH, D_MODEL)),
        'w_router': nrm(ks[17], (DEPTH, D_MODEL, N_EXPERTS), D_MODEL ** -0.5),
        'w_expert_gate': nrm(ks[18], (DEPTH, N_EXPERTS, D_MODEL, D_EXPERT), D_MODEL ** -0.5),
        'w_expert_up': nrm(ks[19], (DEPTH, N_EXPERTS, D_MODEL, D_EXPERT), D_MODEL ** -0.5),
        'w_expert_down': nrm(ks[20], (DEPTH, N_EXPERTS, D_EXPERT, D_MODEL), D_EXPERT ** -0.5),
    }

def reference(x_prompt, x_sample, c_prompt, c_sample, w_ada, b_ada, g_pre_mix, g_post_mix, w_in, b_gates,
              g_mlstm, na_rel_bias, w_out, g_pre_ffn, g_post_ffn, w_router, w_expert_gate, w_expert_up,
              w_expert_down):
    y_prompt = trunk(x_prompt, c_prompt, w_ada, b_ada, g_pre_mix, g_post_mix, w_in, b_gates, g_mlstm, na_rel_bias,
                     w_out, g_pre_ffn, g_post_ffn, w_router, w_expert_gate, w_expert_up, w_expert_down)
    y_sample = trunk(x_sample, c_sample, w_ada, b_ada, g_pre_mix, g_post_mix, w_in, b_gates, g_mlstm, na_rel_bias,
                     w_out, g_pre_ffn, g_post_ffn, w_router, w_expert_gate, w_expert_up, w_expert_down)
    return (y_prompt, y_sample)


_drawn_inputs = setup_inputs


def setup_inputs(seed=0):
    import zlib

    import numpy as np

    out = dict(_drawn_inputs(seed))
    spreads = {}
    factors = {'g_post_ffn': 4.048}
    for name, (base, spread) in spreads.items():
        noise = np.random.default_rng([zlib.crc32(name.encode()), seed]).standard_normal(out[name].shape)
        drawn = base * np.exp(spread * noise) if base else spread * noise
        out[name] = __import__('jax').numpy.asarray(drawn.astype(out[name].dtype))
    for name, factor in factors.items():
        out[name] = (out[name] * factor).astype(out[name].dtype)
    return out
```

```python
import numpy as np
import concourse.bass as bass
from concourse import mybir
from contextlib import ExitStack

F32 = mybir.dt.float32
F32R = mybir.dt.float32r
U32 = mybir.dt.uint32
ALU = mybir.AluOpType
ACT = mybir.ActivationFunctionType
AX = mybir.AxisListType

P = 128
GROUPS = 2
SEQ = 1024
D = 1024
KC = D // P
TT = SEQ // P
HALF = 512
BANKS = 8
EPS = 1e-6
N_MOD = 6
M_HEADS = 4
M_DIM = 128
MW = M_HEADS * M_DIM
A_HEADS = 8
A_DIM = 64
GRID_W = 64
N_EXPERTS = 16
CAP = 2 * SEQ // N_EXPERTS
GATES = 4 * M_HEADS
NEG = -1e30
ONE = 1
SHIFT1, SCALE1, GATE1, SHIFT2, SCALE2, GATE2 = range(N_MOD)


class Space:

    def __init__(self, nc, ctx, stage, words=0):
        self.nc, self.ctx, self.stage = nc, ctx, stage
        self.pool = self.sb("parts", [P, words]) if words else None
        self.taken = 0
        self.used, self.soft = [], []
        ctx.callback(self.clear)

    def start(self):
        nc = self.nc
        engines = (nc.sync, nc.scalar, nc.vector, nc.tensor, nc.gpsimd)
        for i, sem in enumerate(self.used):
            engines[i % len(engines)].drain().then_inc(sem, ONE)
        nc.all_engine_barrier()

    def clear(self):
        self.nc.clear_and_free_semaphores(self.used + self.soft)
        self.nc.all_engine_barrier()

    def part(self, shape, dt=F32):
        n = 1
        for size in shape[1:]:
            n *= size
        cols = self.pool[0:shape[0], self.taken:self.taken + n]
        self.taken += n
        names = "abcd"[:len(shape) - 1]
        cols = cols.rearrange(f"p ({' '.join(names)}) -> p {' '.join(names)}", **dict(zip(names, shape[1:])))
        return cols if dt == F32 else cols.bitcast(dt)

    def sb(self, name, shape, dt=F32):
        return self.ctx.enter_context(self.nc.sbuf_tensor(f"{self.stage}_{name}", shape, dt))

    def ps(self, name, shape, dt=F32):
        return self.ctx.enter_context(self.nc.psum_tensor(f"{self.stage}_{name}", shape, dt))

    def soft_sem(self, name):
        self.soft.append(self.nc.alloc_semaphore(f"{self.stage}_{name}"))
        return self.soft[-1]

    def sem(self, name):
        self.used.append(self.nc.alloc_semaphore(f"{self.stage}_{name}"))
        return self.used[-1]

    def sems(self, name, n):
        return [self.sem(f"{name}{i}") for i in range(n)]


def identity(nc, pool, ident):
    nc.gpsimd.memset(ident[:, :], 0.0)
    pool.drain()
    return nc.gpsimd.affine_select(out=ident[:, :], in_=ident[:, :], compare_op=ALU.not_equal, fill=1.0,
                                   base=0, pattern=[[-1, P]], channel_multiplier=1)


def adaln(nc, io):
    NB = N_MOD * D // HALF
    RING = 4
    w_view = io["w_ada"].rearrange("(k p) (b n) -> b p k n", p=P, n=HALF)
    b_view = io["b_ada"].rearrange("a (b n) -> b a n", n=HALF)
    mod_view = io["mod"].rearrange("g (b n) -> b g n", n=HALF)
    with ExitStack() as ctx:
        s = Space(nc, ctx, "ada")
        c_in = s.sb("c_in", [P, KC, GROUPS])
        c_silu = s.sb("c_silu", [P, KC, GROUPS])
        w = s.sb("w", [P, RING, KC, HALF])
        bias = s.sb("bias", [GROUPS, RING, HALF])
        row = s.sb("row", [GROUPS, RING, HALF])
        acc = s.ps("acc", [GROUPS, RING, HALF])
        c_loaded = s.sem("c_loaded")
        c_ready = s.sem("c_ready")
        w_loaded = s.sems("w_loaded", RING)
        b_loaded = [s.soft_sem(f"b_loaded{j}") for j in range(RING)]
        prod_done = s.sem("prod_done")
        row_done = s.sem("row_done")
        row_stored = s.sems("row_stored", RING)
        s.start()
        block = ctx.enter_context(nc.Block())

        @block.sync
        def _(sp):
            sp.dma_start(c_in[:, :, :], io["c_t"]).then_inc(c_loaded, 16)
            with sp.Fori(0, NB // RING) as i:
                for j in range(RING):
                    sp.wait_ge(prod_done, ONE + i * RING)
                    sp.dma_start(w[:, j, :, :], w_view[i * RING + j]).then_inc(w_loaded[j], 16)

        @block.gpsimd
        def _(pool):
            with pool.Fori(0, NB // RING) as i:
                for j in range(RING):
                    pool.wait_ge(row_done, ONE + i * RING)
                    pool.dma_start(bias[:, j, :], b_view[i * RING + j].to_broadcast([GROUPS, HALF])).then_inc(b_loaded[j], 16)

        @block.scalar
        def _(act):
            act.wait_ge(c_loaded, ONE + 16)
            nc.scalar.activation(c_silu[:, :, :], c_in[:, :, :], ACT.Silu).then_inc(c_ready, 1)
            with act.Fori(0, NB // RING) as i:
                for j in range(RING):
                    act.wait_ge(row_done, ONE + i * RING + j + 1)
                    act.dma_start(mod_view[i * RING + j], row[:, j, :]).then_inc(row_stored[j], 16)
            for j in range(RING):
                act.wait_ge(row_stored[j], ONE + 16 * (NB // RING))

        @block.tensor
        def _(pe):
            pe.wait_ge(c_ready, ONE + 1)
            with pe.Fori(0, NB // RING) as i:
                for j in range(RING):
                    pe.wait_ge(w_loaded[j], ONE + 16 * i + 16)
                    pe.wait_ge(row_done, ONE + i * RING)
                    for k in range(KC):
                        mm = nc.tensor.matmul(acc[:, j, :], c_silu[:, k, :], w[:, j, k, :],
                                              start=(k == 0), stop=(k == KC - 1))
                    mm.then_inc(prod_done, 1)

        @block.vector
        def _(dve):
            with dve.Fori(0, NB // RING) as i:
                for j in range(RING):
                    dve.wait_ge(b_loaded[j], 16 * i + 16)
                    dve.wait_ge(row_stored[j], ONE + 16 * i)
                    dve.wait_ge(prod_done, ONE + i * RING + j + 1)
                    nc.vector.tensor_tensor(row[:, j, :], acc[:, j, :], bias[:, j, :], ALU.add).then_inc(row_done, 1)


def projections(nc, io):
    UNITS = 8
    FM = 4
    TM = 3
    BLK = HALF // P * 2
    PER_G = (FM + TM) * BLK + 2
    STAGES = 4
    HB = KC * 2
    x_view = io["x"].rearrange("(g t p) n -> g p t n", g=GROUPS, p=P)
    sh_view = io["mod"].rearrange("g (m k p) -> g m p k", m=N_MOD, p=P)
    fm_view = io["qk_t"].rearrange("u (g f p) (t n) -> g u f t p n", g=GROUPS, p=P, n=HALF)
    tm_view = io["vov"].rearrange("u (g h) (t p) n -> g u t p h n", g=GROUPS, p=P)
    gates_view = io["gates_t"].rearrange("g c (t n) -> g t c n", n=HALF)
    with ExitStack() as ctx:
        s = Space(nc, ctx, "prj")
        x = s.sb("x", [P, TT, D])
        junk = s.sb("junk", [P, D])
        ss = s.sb("ss", [P, TT])
        mhalf = s.sb("mhalf", [P, TT])
        rms = s.sb("rms", [P, TT])
        ident = s.sb("ident", [P, P])
        g_pre = s.sb("g_pre", [P, KC])
        mods = s.sb("mods", [P, 2, KC])
        scale = s.sb("scale", [P, KC])
        hf = s.sb("hf", [P, 2, HALF])
        h_hi = s.sb("h_hi", [P, KC, SEQ], F32R)
        h_lo = s.sb("h_lo", [P, KC, SEQ], F32R)
        wf = s.sb("wf", [P, 2, KC, HALF // 2])
        w_hi = s.sb("w_hi", [P, 2, KC, HALF], F32R)
        w_lo = s.sb("w_lo", [P, 2, KC, HALF], F32R)
        stage = s.sb("stage", [P, STAGES, HALF])
        acc = s.ps("acc", [P, BANKS, HALF])

        x_loaded = s.sem("x_loaded")
        g_loaded = s.sem("g_loaded")
        mods_loaded = s.sem("mods_loaded")
        ident_ready = s.sem("ident_ready")
        ss_ready = s.sem("ss_ready")
        mean_ready = s.sem("mean_ready")
        rms_ready = s.sem("rms_ready")
        scale_ready = s.sem("scale_ready")
        xn_ready = s.sem("xn_ready")
        turned = s.sem("turned")
        hf_ready = s.sem("hf_ready")
        h_ready = s.sem("h_ready")
        w_loaded = s.sems("w_loaded", 2)
        w_hi_ready = s.sem("w_hi_ready")
        w_lo_ready = s.sem("w_lo_ready")
        blk_done = s.sem("blk_done")
        evac_done = s.sem("evac_done")
        stored = s.sems("stored", STAGES)
        s.start()
        block = ctx.enter_context(nc.Block())

        def uses(slot):
            return len(range(slot, PER_G, STAGES))

        def width(u):
            return GATES if u == UNITS - 1 else HALF

        def w_cols(u):
            return [(0, GATES // 2), (GATES // 2, GATES // 2)] if u == UNITS - 1 else [(0, HALF // 2), (HALF // 2, HALF // 2)]

        @block.sync
        def _(sp):
            sp.dma_start(g_pre[:, :], io["g_pre_mix"]).then_inc(g_loaded, 16)

            def load(g, u, su):
                for h, (c0, cw) in enumerate(w_cols(su)):
                    sp.wait_ge(w_lo_ready, ONE + ((g * UNITS + u) * 2 - 1 + h if su or h else (g * UNITS + u) * 2))
                    src = io["w_gates"][:, :, c0:c0 + cw] if su == UNITS - 1 else io["w_units"][u, :, :, c0:c0 + cw]
                    sp.dma_start(wf[:, h, :, 0:cw], src).then_inc(w_loaded[h], 16)

            with sp.Fori(0, GROUPS) as g:
                sp.wait_ge(turned, ONE + g * HB)
                sp.dma_start(x[:, :, :], x_view[g]).then_inc(x_loaded, 16)
                sp.wait_ge(scale_ready, ONE + g)
                sp.wait_ge(hf_ready, ONE + g * HB)
                sp.dma_start(mods[:, 0, :], sh_view[g, SHIFT1], allow_slow_non_contiguous=True).then_inc(mods_loaded, 16)
                sp.dma_start(mods[:, 1, :], sh_view[g, SCALE1], allow_slow_non_contiguous=True).then_inc(mods_loaded, 16)
                load(g, 0, 0)

                def store(slot, m, dst, rows):
                    sp.wait_ge(evac_done, ONE + g * PER_G + m + 1)
                    src = stage[0:rows, slot, :]
                    if len(dst.shape) == 3:
                        src = src.rearrange("p (h n) -> p h n", n=P)
                    sp.dma_start(dst, src).then_inc(stored[slot], 16)

                with sp.Fori(0, FM) as u:
                    load(g, u + 1, 1)
                    for b in range(BLK):
                        store(b % STAGES, u * BLK + b, fm_view[g, u, b // 2, b % 2], P)
                for u in range(FM, FM + TM):
                    load(g, u + 1, u + 1)
                    for b in range(BLK):
                        store(b % STAGES, u * BLK + b, tm_view[g, u - FM, b], P)
                for b in range(2):
                    store(b, PER_G - 2 + b, gates_view[g, b], GATES)
            for slot in range(STAGES):
                sp.wait_ge(stored[slot], ONE + 16 * GROUPS * uses(slot))

        @block.gpsimd
        def _(pool):
            identity(nc, pool, ident).then_inc(ident_ready, 1)
            nc.gpsimd.memset(mhalf[:, :], -0.5)
            pool.drain()
            with pool.Fori(0, GROUPS) as g:
                pool.wait_ge(mean_ready, ONE + g + 1)
                nc.gpsimd.tensor_tensor(rms[:, :], ss[:, :], mhalf[:, :], ALU.pow).then_inc(rms_ready, 1)

        @block.scalar
        def _(act):
            def split_hi(g, u, su):
                for h, (c0, cw) in enumerate(w_cols(su)):
                    act.wait_ge(w_loaded[h], ONE + (g * UNITS + u) * 16 + 16)
                    if h == 0:
                        act.wait_ge(blk_done, ONE + (g * PER_G + (u - 1) * BLK if su else g * PER_G))
                    nc.scalar.activation(w_hi[:, slot_of(su), :, c0:c0 + cw], wf[:, h, :, 0:cw], ACT.Copy).then_inc(w_hi_ready, 1)

            def slot_of(su):
                return su % 2

            def evac(g, slot, bank, m, k, rows):
                act.wait_ge(blk_done, ONE + g * PER_G + m + 1)
                act.wait_ge(stored[slot], ONE + 16 * (g * uses(slot) + k))
                nc.scalar.activation(stage[0:rows, slot, :], acc[0:rows, bank, :], ACT.Copy).then_inc(evac_done, 1)

            with act.Fori(0, GROUPS) as g:
                act.drain()
                act.wait_ge(x_loaded, ONE + 16 * g + 16)
                act.wait_ge(mean_ready, ONE + g)
                act.wait_ge(rms_ready, ONE + g)
                for t in range(TT):
                    if t:
                        act.drain()
                    nc.scalar.activation(junk[:, :], x[:, t, :], ACT.Square, accum_out=ss[:, t:t + 1]).then_inc(ss_ready, 1)
                act.wait_ge(scale_ready, ONE + g + 1)
                for b in range(HB):
                    act.wait_ge(turned, ONE + g * HB + b + 1)
                    if b >= 2:
                        act.wait_ge(h_ready, ONE + g * HB + b - 1)
                    else:
                        act.wait_ge(h_ready, ONE + g * HB)
                    k = b // 2
                    nc.scalar.activation(hf[:, b % 2, :], acc[:, b % BANKS, :], ACT.Identity,
                                         scale=scale[:, k:k + 1], bias=mods[:, 0, k:k + 1]).then_inc(hf_ready, 1)
                split_hi(g, 0, 0)
                with act.Fori(0, FM // 2) as up:
                    for j in range(2):
                        u = up * 2 + j
                        split_hi(g, u + 1, 1 + j)
                        for b in range(BLK):
                            evac(g, b % STAGES, b, u * BLK + b, u * (BLK // STAGES) + b // STAGES, P)
                for u in range(FM, FM + TM):
                    split_hi(g, u + 1, u + 1)
                    for b in range(BLK):
                        evac(g, b % STAGES, b, u * BLK + b, u * (BLK // STAGES) + b // STAGES, P)
                for b in range(2):
                    evac(g, b, b, PER_G - 2 + b, (FM + TM) * (BLK // STAGES), GATES)

        @block.vector
        def _(dve):
            def split_lo(g, u, su):
                for h, (c0, cw) in enumerate(w_cols(su)):
                    dve.wait_ge(w_hi_ready, ONE + (g * UNITS + u) * 2 + h + 1)
                    hi = w_hi[:, su % 2, :, c0:c0 + cw]
                    nc.vector.tensor_tensor(w_lo[:, su % 2, :, c0:c0 + cw], wf[:, h, :, 0:cw], hi.bitcast(F32), ALU.subtract).then_inc(w_lo_ready, 1)

            dve.wait_ge(g_loaded, ONE + 16)
            with dve.Fori(0, GROUPS) as g:
                dve.wait_ge(mods_loaded, ONE + 32 * g + 32)
                nc.vector.scalar_tensor_tensor(scale[:, :], mods[:, 1, :], 1.0, g_pre[:, :], ALU.add, ALU.mult).then_inc(scale_ready, 1)
                dve.wait_ge(ss_ready, ONE + g * TT + TT)
                nc.vector.tensor_scalar(ss[:, :], ss[:, :], 1.0 / D, EPS, ALU.mult, ALU.add).then_inc(mean_ready, 1)
                dve.wait_ge(rms_ready, ONE + g + 1)
                for t in range(TT):
                    nc.vector.tensor_scalar(x[:, t, :], x[:, t, :], rms[:, t:t + 1], None, ALU.mult).then_inc(xn_ready, 1)
                dve.wait_ge(blk_done, ONE + g * PER_G)
                for b in range(HB):
                    dve.wait_ge(hf_ready, ONE + g * HB + b + 1)
                    k, c = b // 2, (b % 2) * HALF
                    nc.vector.tensor_copy(h_hi[:, k, c:c + HALF], hf[:, b % 2, :])
                    dve.drain()
                    nc.vector.tensor_tensor(h_lo[:, k, c:c + HALF], hf[:, b % 2, :], h_hi[:, k, c:c + HALF].bitcast(F32), ALU.subtract).then_inc(h_ready, 1)
                split_lo(g, 0, 0)
                with dve.Fori(0, FM // 2) as up:
                    for j in range(2):
                        split_lo(g, up * 2 + j + 1, 1 + j)
                for u in range(FM, FM + TM):
                    split_lo(g, u + 1, u + 1)

        @block.tensor
        def _(pe):
            pe.wait_ge(ident_ready, ONE + 1)

            def three_passes(bank, rows, lhs, rhs):
                for k in range(KC):
                    for i, (a, b) in enumerate(((0, 0), (0, 1), (1, 0))):
                        mm = nc.tensor.matmul(acc[0:rows, bank, :], lhs(a, k), rhs(b, k),
                                              start=(k == 0 and i == 0), stop=(k == KC - 1 and i == 2))
                return mm

            h = (h_hi, h_lo)
            w = (w_hi, w_lo)

            def unit(g, u, su):
                pe.wait_ge(h_ready, ONE + g * HB + HB)
                pe.wait_ge(w_lo_ready, ONE + (g * UNITS + u) * 2 + 2)
                for b in range(2 if su == UNITS - 1 else BLK):
                    if su == 0:
                        pe.wait_ge(evac_done, ONE + g * PER_G + u * BLK)
                    else:
                        pe.wait_ge(evac_done, ONE + g * PER_G + (u - 1) * BLK + b + 1)
                    if su < FM:
                        f, t = b // 2, b % 2
                        mm = three_passes(b, P, lambda a, k: w[a][:, su % 2, k, f * P:f * P + P],
                                          lambda a, k: h[a][:, k, t * HALF:(t + 1) * HALF])
                    elif su < FM + TM:
                        mm = three_passes(b, P, lambda a, k: h[a][:, k, b * P:b * P + P],
                                          lambda a, k: w[a][:, su % 2, k, :])
                    else:
                        mm = three_passes(b, GATES, lambda a, k: w[a][:, su % 2, k, 0:GATES],
                                          lambda a, k: h[a][:, k, b * HALF:(b + 1) * HALF])
                    mm.then_inc(blk_done, 1)

            with pe.Fori(0, GROUPS) as g:
                pe.wait_ge(evac_done, ONE + g * PER_G)
                for b in range(HB):
                    k, c = b // 2, b % 2
                    if b >= BANKS:
                        pe.wait_ge(hf_ready, ONE + g * HB + b - BANKS + 1)
                    for j in range(HALF // P):
                        t = c * (HALF // P) + j
                        if b < 2:
                            pe.wait_ge(xn_ready, ONE + g * TT + t + 1)
                        mm = nc.tensor.transpose(acc[:, b % BANKS, j * P:j * P + P], x[:, t, k * P:k * P + P], ident[:, :])
                    mm.then_inc(turned, 1)
                with pe.Fori(0, FM // 2) as up:
                    for j in range(2):
                        unit(g, up * 2 + j, j)
                for u in range(FM, UNITS):
                    unit(g, u, u)


def mlstm(nc, io):
    NH = GROUPS * M_HEADS
    C = SEQ // P
    R = 32 + NH
    BWD = 32
    V1 = M_DIM + 2
    QU, QW, QI, QE = range(4)
    K_SCALE = float(M_DIM) ** -0.5
    STEPS = C
    vov = io["vov"].rearrange("u n (c p) d -> u n p c d", p=P)
    qk = io["qk_t"].rearrange("u (n p) t -> u n p t", p=P)
    mix = io["mix_t"]
    with ExitStack() as ctx:
        s = Space(nc, ctx, "ml", words=37 * SEQ)
        ident = s.part([P, P])
        mask = s.part([P, 2, P])
        bias = s.part([R, 2])
        li = s.part([R, SEQ])
        fr = s.part([R, SEQ])
        t1 = s.part([R, SEQ])
        keep = s.part([R, SEQ])
        drop = s.part([R, SEQ])
        b = s.part([R, SEQ])
        m = s.part([R, SEQ])
        quant = [s.part([R, SEQ]) for i in range(3)]
        G = s.part([R, C])
        mend = s.part([R, C])
        mn = s.part([R, C])
        ms = s.part([R, C])
        gm = s.part([R, C])
        so = s.part([R, C])
        cols = s.part([P, 4, C, 64])
        g_cols = s.part([P, NH])
        half_neg = s.part([P, C])
        qT = s.part([P, 2, SEQ])
        kT = s.part([P, 2, SEQ])
        v1 = s.part([P, 2, C, V1])
        og = s.part([P, 2, C, M_DIM])
        E = s.part([P, 2, 2, SEQ])
        sold = s.part([P, 2, 2, C])
        col = s.part([P, 2, 4, C, 2])
        gcol = s.part([P, 2])
        kt = s.part([P, SEQ])
        kw = s.part([P, 2, C, M_DIM])
        cst = s.part([P, 2, 2, V1])
        inter = s.part([P, 2, 2, V1])
        nd = s.part([P, 2 * C, V1])
        rr = s.part([P, 2 * C])
        r1 = s.part([P, 2 * C])
        hb = s.part([P, C, M_DIM])
        hf = s.part([P, C, M_DIM])
        hn = s.part([P, 2, C, M_DIM])
        ss = s.part([P, C])
        r2 = s.part([P, C])
        outT = s.part([P, 2, SEQ])
        pKS = s.ps("pKS", [P, 2, HALF])
        pC = s.ps("pC", [P, 2, HALF])
        pA = s.ps("pA", [P, 2, HALF])
        pB = s.ps("pB", [P, 2, HALF])

        zeroed = s.sem("zeroed")
        g_loaded = s.sem("g_loaded")
        pool_ready = s.sem("pool_ready")
        dve_step = s.sem("dve_step")
        act_step = s.sem("act_step")
        rows_ready = s.sem("rows_ready")
        rows_stored = s.sem("rows_stored")
        cols_turned = s.sem("cols_turned")
        cols_ready = s.sem("cols_ready")
        qk_loaded = s.sems("qk_loaded", 2)
        v_loaded = s.sems("v_loaded", 2)
        o_loaded = s.sems("o_loaded", 2)
        e_loaded = s.sems("e_loaded", 2)
        arg_ready = s.sem("arg_ready")
        exp_ready = s.sem("exp_ready")
        mask_ready = s.sem("mask_ready")
        k_turned = s.sem("k_turned")
        kt_ready = s.sem("kt_ready")
        kw_ready = s.sem("kw_ready")
        s_done = s.sem("s_done")
        sf_ready = s.sem("sf_ready")
        c_done = s.sem("c_done")
        a_done = s.sem("a_done")
        b_done = s.sem("b_done")
        cst_ready = s.sem("cst_ready")
        inter_ready = s.sem("inter_ready")
        nd_ready = s.sem("nd_ready")
        rr_ready = s.sem("rr_ready")
        hb_ready = s.sem("hb_ready")
        hf_ready = s.sem("hf_ready")
        sq_ready = s.sem("sq_ready")
        mean_ready = s.sem("mean_ready")
        r2_ready = s.sem("r2_ready")
        og_ready = s.sem("og_ready")
        hn_ready = s.sem("hn_ready")
        o_turned = s.sem("o_turned")
        out_ready = s.sem("out_ready")
        out_stored = s.sems("out_stored", 2)
        s.start()
        block = ctx.enter_context(nc.Block())

        def over_heads(eng, body):
            with eng.Fori(0, NH // 2 - 1) as i:
                for j in range(2):
                    body(i * 2 + j, j, False)
            for j in range(2):
                body(NH - 2 + j, j, j == 1)

        @block.sync
        def _(sp):
            sp.wait_ge(zeroed, ONE + 1)
            for d in range(2):
                for g in range(GROUPS):
                    for i, rows in enumerate((li, fr)):
                        r0 = d * BWD + g * M_HEADS
                        c0 = (d * 2 + i) * M_HEADS
                        sp.dma_start(rows[r0:r0 + M_HEADS, :], io["gates_t"][g, c0:c0 + M_HEADS, :]).then_inc(g_loaded, 16)
            sp.dma_start(bias[:, :], io["b_gates"]).then_inc(g_loaded, 16)
            sp.dma_start(g_cols[:, :], io["g_mlstm"]).then_inc(g_loaded, 16)
            sp.wait_ge(rows_ready, ONE + 2)
            sp.dma_start(io["nmx"], t1[:, :]).then_inc(rows_stored, 16)
            sp.dma_start(io["sold"], so[:, :]).then_inc(rows_stored, 16)
            sp.wait_ge(rows_stored, ONE + 32)

            def load(n, j, first=False):
                if not first:
                    sp.wait_ge(hn_ready, ONE + n - 1)
                sp.dma_start(qT[:, j, :], qk[0, n]).then_inc(qk_loaded[j], 16)
                sp.dma_start(kT[:, j, :], qk[1, n]).then_inc(qk_loaded[j], 16)
                for d in range(2):
                    sp.dma_start(E[:, j, d, :], io["nmx"][bass.ds(n + d * BWD, 1), :].to_broadcast([P, SEQ])).then_inc(e_loaded[j], 16)
                    sp.dma_start(sold[:, j, d, :], io["sold"][bass.ds(n + d * BWD, 1), :].to_broadcast([P, C])).then_inc(e_loaded[j], 16)
                sp.dma_start(v1[:, j, :, 0:M_DIM], vov[0, n]).then_inc(v_loaded[j], 16)
                sp.dma_start(og[:, j, :, :], vov[1, n]).then_inc(o_loaded[j], 16)

            load(0, 0, True)
            load(1, 1, True)

            def head(n, j, last):
                sp.wait_ge(out_ready, ONE + n + 1)
                sp.dma_start(mix[0, n], outT[:, j, :]).then_inc(out_stored[j], 16)

            with sp.Fori(0, NH // 2 - 1) as i:
                for j in range(2):
                    load(i * 2 + j + 2, j)
                    head(i * 2 + j, j, False)
            for j in range(2):
                head(NH - 2 + j, j, False)
            for j in range(2):
                sp.wait_ge(out_stored[j], ONE + 16 * NH // 2)

        @block.gpsimd
        def _(pool):
            for rows in (li, fr, b, m):
                nc.gpsimd.memset(rows[:, :], 0.0)
            for rows in (G, mend, mn, ms):
                nc.gpsimd.memset(rows[:, :], 0.0)
            nc.gpsimd.memset(keep[:, :], 1.0)
            pool.drain()
            nc.gpsimd.memset(keep[0:NH, 0:SEQ:P], 0.0).then_inc(zeroed, 1)
            pool.drain()
            nc.gpsimd.memset(keep[BWD:R, P - 1:SEQ:P], 0.0)
            pool.drain()
            nc.gpsimd.memset(half_neg[:, :], -0.5)
            nc.gpsimd.memset(v1[:, :, :, M_DIM:V1], 1.0)
            nc.gpsimd.memset(mask[:, :, :], 1.0)
            identity(nc, pool, ident)
            for d in range(2):
                sign = 1 - 2 * d
                nc.gpsimd.affine_select(out=mask[:, d, :], in_=mask[:, d, :], compare_op=ALU.is_ge, fill=0.0, base=0,
                                        pattern=[[sign, P]], channel_multiplier=-sign)
            pool.drain()
            nc.gpsimd.memset(r2[:, 0:1], 0.0).then_inc(pool_ready, 1)

            def head_masks(n, j):
                pool.wait_ge(exp_ready, ONE + n + 1)
                for d in range(2):
                    view = E[:, j, d, :].rearrange("p (c t) -> p c t", t=P)
                    nc.gpsimd.tensor_tensor(view, view, mask[:, d:d + 1, :].to_broadcast([P, C, P]), ALU.mult).then_inc(mask_ready, 1)

            def head_kw(n, j):
                pool.wait_ge(kt_ready, ONE + 2 * n + 2)
                pool.wait_ge(arg_ready, ONE + n + 1)
                for d in range(2):
                    a = nc.gpsimd.tensor_tensor(kw[:, d, :, :], kt[:, :].rearrange("p (c t) -> p c t", t=P),
                                                col[:, j, QW, :, d].unsqueeze(2).to_broadcast([P, C, M_DIM]), ALU.mult)
                a.then_inc(kw_ready, 1)

            def head_post(n, j):
                pool.wait_ge(rr_ready, ONE + n + 1)
                nc.gpsimd.tensor_tensor(hb[:, :, :], nd[:, C:2 * C, 0:M_DIM], rr[:, C:2 * C].unsqueeze(2).to_broadcast([P, C, M_DIM]), ALU.mult).then_inc(hb_ready, 1)
                pool.wait_ge(mean_ready, ONE + n + 1)
                nc.gpsimd.tensor_tensor(r2[:, :], ss[:, :], half_neg[:, :], ALU.pow).then_inc(r2_ready, 1)

            head_masks(0, 0)
            head_kw(0, 0)

            def body(n, j, last):
                if not last:
                    head_masks(n + 1, 1 - j)
                    pool.wait_ge(c_done, ONE + (n + 1) * (STEPS - 1))
                    head_kw(n + 1, 1 - j)
                head_post(n, j)

            over_heads(pool, body)

        @block.scalar
        def _(act):
            act.wait_ge(dve_step, ONE + 1)
            nc.scalar.activation(t1[:, :], t1[:, :], ACT.Exp)
            act.drain()
            nc.scalar.activation(t1[:, :], t1[:, :], ACT.Ln, bias=1.0).then_inc(act_step, 1)
            act.wait_ge(dve_step, ONE + 2)
            nc.scalar.activation(so[:, :], so[:, :], ACT.Exp)
            nc.scalar.activation(quant[0][:, :], quant[0][:, :], ACT.Exp)
            nc.scalar.activation(quant[1][:, :], quant[1][:, :], ACT.Exp)
            nc.scalar.activation(quant[2][:, :], quant[2][:, :], ACT.Exp, scale=-1.0).then_inc(rows_ready, 1)
            for q, bank in enumerate((pC, pC, pA, pA)):
                act.wait_ge(cols_turned, ONE + q + 1)
                nc.scalar.activation(cols[:, q, :, 0:R], bank[:, q % 2, 0:C * R].rearrange("p (c r) -> p c r", r=R), ACT.Copy,
                                     scale=K_SCALE if q == QW else 1.0).then_inc(cols_ready, 1)

            def head_exp(n, j):
                act.wait_ge(arg_ready, ONE + n + 1)
                nc.scalar.activation(E[:, j, :, :], E[:, j, :, :], ACT.Exp).then_inc(exp_ready, 1)

            def head_kt(n, j, first=False):
                for half in range(2):
                    act.wait_ge(k_turned, ONE + 2 * n + half + 1)
                    if half == 0 and not first:
                        act.wait_ge(kw_ready, ONE + n)
                    nc.scalar.activation(kt[:, half * HALF:(half + 1) * HALF], pKS[:, half, :], ACT.Copy).then_inc(kt_ready, 1)

            def head_steps(n, j):
                for i in range(1, STEPS):
                    k = i - 1
                    act.wait_ge(b_done, ONE + n * (STEPS - 1) + k + 1)
                    act.wait_ge(nd_ready, ONE + n * STEPS + i - 1)
                    for d, c in ((0, i), (1, C - 1 - i)):
                        a = nc.scalar.activation(inter[:, i % 2, d, :], pB[:, i % 2, d * V1:(d + 1) * V1], ACT.Copy,
                                                 scale=col[:, j, QI, c, d:d + 1])
                    a.then_inc(inter_ready, 1)

            def head_post(n, j):
                act.wait_ge(o_loaded[j], ONE + (n - j) * 8 + 16)
                nc.scalar.activation(og[:, j, :, :], og[:, j, :, :], ACT.Sigmoid).then_inc(og_ready, 1)
                act.wait_ge(hf_ready, ONE + n + 1)
                nc.scalar.activation(hb[:, :, :], hf[:, :, :], ACT.Square).then_inc(sq_ready, 1)

            def head_out(n, j, first=False):
                if not first:
                    act.wait_ge(out_stored[j], ONE + (n - j) * 8)
                for half in range(2):
                    act.wait_ge(o_turned, ONE + 2 * n + half + 1)
                    a = nc.scalar.activation(outT[:, j, half * HALF:(half + 1) * HALF], pB[:, half, :], ACT.Copy, scale=gcol[:, j:j + 1])
                a.then_inc(out_ready, 1)

            head_exp(0, 0)
            head_kt(0, 0, True)

            def body(n, j, last):
                if not last:
                    head_exp(n + 1, 1 - j)
                    head_kt(n + 1, 1 - j)
                head_steps(n, j)
                head_post(n, j)
                head_out(n, j)

            over_heads(act, body)

        @block.vector
        def _(dve):
            dve.wait_ge(pool_ready, ONE + 1)
            dve.wait_ge(g_loaded, ONE + 16 * 10)
            nc.vector.tensor_scalar(li[:, :], li[:, :], bias[:, 0:1], None, ALU.add)
            nc.vector.tensor_scalar(fr[:, :], fr[:, :], bias[:, 1:2], None, ALU.add)
            nc.vector.tensor_scalar(drop[:, :], keep[:, :], -1.0, -NEG, ALU.add, ALU.mult)
            dve.drain()
            nc.vector.scalar_tensor_tensor(t1[:, :], fr[:, :], -1.0, fr[:, :], ALU.mult, ALU.min).then_inc(dve_step, 1)
            dve.wait_ge(act_step, ONE + 1)
            nc.vector.scalar_tensor_tensor(fr[:, :], fr[:, :], 0.0, t1[:, :], ALU.min, ALU.subtract)
            dve.drain()
            for r0, rev in ((0, slice(None)), (BWD, slice(None, None, -1))):
                rows = slice(r0, r0 + NH)
                nc.vector.tensor_tensor_scan(b[rows, rev], keep[rows, rev], fr[rows, rev], 0.0, ALU.mult, ALU.add)
            dve.drain()
            u = li
            nc.vector.tensor_tensor(u[:, :], li[:, :], b[:, :], ALU.subtract)
            dve.drain()
            for r0, rev in ((0, slice(None)), (BWD, slice(None, None, -1))):
                rows = slice(r0, r0 + NH)
                nc.vector.tensor_tensor_scan(m[rows, rev], drop[rows, rev], u[rows, rev], 0.0, ALU.add, ALU.max)
            dve.drain()
            for r0, end in ((0, P - 1), (BWD, 0)):
                rows = slice(r0, r0 + NH)
                nc.vector.tensor_copy(G[rows, :], b[rows, end:SEQ:P])
                nc.vector.tensor_copy(mend[rows, :], m[rows, end:SEQ:P])
            dve.drain()
            nc.vector.tensor_tensor(mend[:, :], G[:, :], mend[:, :], ALU.add)
            dve.drain()
            for r0, rev in ((0, slice(None)), (BWD, slice(None, None, -1))):
                rows = slice(r0, r0 + NH)
                nc.vector.tensor_tensor_scan(mn[rows, rev], G[rows, rev], mend[rows, rev], 0.0, ALU.add, ALU.max)
            dve.drain()
            nc.vector.tensor_copy(ms[0:NH, 1:C], mn[0:NH, 0:C - 1])
            nc.vector.tensor_copy(ms[BWD:R, 0:C - 1], mn[BWD:R, 1:C])
            nc.vector.tensor_tensor(gm[:, :], G[:, :], mn[:, :], ALU.subtract)
            dve.drain()
            nc.vector.tensor_tensor(so[:, :], gm[:, :], ms[:, :], ALU.add)
            chunked = lambda t: t[:, :].rearrange("r (c t) -> r c t", t=P)
            spread = lambda t: t[:, :].unsqueeze(2).to_broadcast([R, C, P])
            nc.vector.tensor_tensor(chunked(m), chunked(m), spread(ms), ALU.max)
            nc.vector.tensor_tensor(chunked(quant[0]), chunked(u), spread(gm), ALU.add)
            dve.drain()
            nc.vector.tensor_tensor(chunked(quant[1]), spread(ms), chunked(m), ALU.subtract)
            nc.vector.tensor_tensor(quant[2][:, :], b[:, :], m[:, :], ALU.add).then_inc(dve_step, 1)
            nc.vector.tensor_scalar(t1[:, :], m[:, :], -1.0, None, ALU.mult).then_inc(rows_ready, 1)

            def head_args(n, j, first=False):
                if not first:
                    dve.wait_ge(out_ready, ONE + n - 1)
                for d in range(2):
                    nc.vector.tensor_copy(col[:, j, :, :, d], cols[:, :, :, bass.ds(n + d * BWD, 1)].squeeze(3))
                nc.vector.tensor_copy(gcol[:, j:j + 1], g_cols[:, bass.ds(n, 1)])
                dve.drain()
                dve.wait_ge(e_loaded[j], ONE + (n - j) * 32 + 64)
                for c in range(C):
                    for d in range(2):
                        e = E[:, j, d, c * P:c * P + P]
                        a = nc.vector.tensor_scalar(e, e, col[:, j, QU, c, d:d + 1], 0.0, ALU.add, ALU.min)
                a.then_inc(arg_ready, 1)

            def head_sf(n, j):
                dve.wait_ge(mask_ready, ONE + 2 * n + 2)
                for half in range(2):
                    dve.wait_ge(s_done, ONE + 2 * n + half + 1)
                    for d in range(2):
                        e = E[:, j, d, half * HALF:(half + 1) * HALF]
                        a = nc.vector.scalar_tensor_tensor(e, pKS[:, half, :], K_SCALE, e, ALU.mult, ALU.mult)
                    a.then_inc(sf_ready, 1)

            def head_steps(n, j):
                for i in range(STEPS):
                    if i:
                        dve.drain()
                        dve.wait_ge(c_done, ONE + n * (STEPS - 1) + i)
                        dve.wait_ge(b_done, ONE + n * (STEPS - 1) + max(i - 2, 0))
                        for d, c in ((0, i - 1), (1, C - i)):
                            new, old = cst[:, i % 2, d, :], cst[:, (i - 1) % 2, d, :]
                            loc = pC[:, i % 2, d * V1:(d + 1) * V1]
                            if i == 1:
                                a = nc.vector.tensor_copy(new, loc)
                            else:
                                a = nc.vector.scalar_tensor_tensor(new, old, sold[:, j, d, c:c + 1], loc, ALU.mult, ALU.add)
                        a.then_inc(cst_ready, 1)
                    dve.wait_ge(a_done, ONE + n * STEPS + i + 1)
                    both = nd[:, i:2 * C - i:2 * C - 1 - 2 * i, :]
                    pa = pA[:, i % 2, 0:2 * V1].rearrange("p (d v) -> p d v", v=V1)
                    if i:
                        dve.wait_ge(inter_ready, ONE + n * (STEPS - 1) + i)
                        nc.vector.tensor_tensor(both, pa, inter[:, i % 2, :, :], ALU.add).then_inc(nd_ready, 1)
                    else:
                        nc.vector.tensor_copy(both, pa).then_inc(nd_ready, 1)

            def head_post(n, j):
                dve.drain()
                den = nd[:, :, M_DIM]
                nc.vector.scalar_tensor_tensor(r1[:, :], den, -1.0, den, ALU.mult, ALU.max)
                dve.drain()
                emo = col[:, j, QE, :, :].rearrange("p c d -> p d c")
                r1v = r1[:, :].rearrange("p (d c) -> p d c", d=2)
                nc.vector.tensor_tensor(r1v, r1v, emo, ALU.max)
                dve.drain()
                nc.vector.reciprocal(rr[:, :], r1[:, :]).then_inc(rr_ready, 1)
                dve.drain()
                nc.vector.tensor_tensor(hf[:, :, :], nd[:, 0:C, 0:M_DIM], rr[:, 0:C].unsqueeze(2).to_broadcast([P, C, M_DIM]), ALU.mult)
                dve.drain()
                dve.wait_ge(hb_ready, ONE + n + 1)
                nc.vector.tensor_tensor(hf[:, :, :], hf[:, :, :], hb[:, :, :], ALU.add).then_inc(hf_ready, 1)
                dve.wait_ge(sq_ready, ONE + n + 1)
                nc.vector.tensor_reduce(ss[:, :], hb[:, :, :], AX.X, ALU.add)
                dve.drain()
                nc.vector.tensor_scalar(ss[:, :], ss[:, :], 1.0 / M_DIM, EPS, ALU.mult, ALU.add).then_inc(mean_ready, 1)
                dve.wait_ge(og_ready, ONE + n + 1)
                dve.wait_ge(o_turned, ONE + 2 * n)
                nc.vector.tensor_tensor(og[:, j, :, :], hf[:, :, :], og[:, j, :, :], ALU.mult)
                dve.drain()
                dve.wait_ge(r2_ready, ONE + n + 1)
                nc.vector.tensor_tensor(hn[:, j, :, :], og[:, j, :, :], r2[:, :].unsqueeze(2).to_broadcast([P, C, M_DIM]), ALU.mult).then_inc(hn_ready, 1)

            dve.wait_ge(cols_ready, ONE + 4)
            head_args(0, 0, True)
            head_sf(0, 0)

            def body(n, j, last):
                if not last:
                    head_args(n + 1, 1 - j)
                head_steps(n, j)
                head_post(n, j)
                if not last:
                    head_sf(n + 1, 1 - j)

            over_heads(dve, body)

        @block.tensor
        def _(pe):
            pe.wait_ge(pool_ready, ONE + 1)
            pe.wait_ge(dve_step, ONE + 2)
            pe.wait_ge(rows_ready, ONE + 2)
            for q, (rows, bank) in enumerate(zip((li, quant[0], quant[1], quant[2]), (pC, pC, pA, pA))):
                for c in range(C):
                    mm = nc.tensor.transpose(bank[:, q % 2, c * R:(c + 1) * R], rows[:, c * P:(c + 1) * P], ident[0:R, 0:R])
                mm.then_inc(cols_turned, 1)

            def head_k(n, j):
                pe.wait_ge(qk_loaded[j], ONE + (n - j) * 16 + 32)
                for half in range(2):
                    for c in range(C // 2):
                        k = half * (C // 2) + c
                        mm = nc.tensor.transpose(pKS[:, half, c * P:(c + 1) * P], kT[:, j, k * P:(k + 1) * P], ident[:, :])
                    mm.then_inc(k_turned, 1)

            def head_s(n, j):
                pe.wait_ge(kt_ready, ONE + 2 * n + 2)
                for half in range(2):
                    for c in range(C // 2):
                        k = half * (C // 2) + c
                        mm = nc.tensor.matmul(pKS[:, half, c * P:(c + 1) * P], kT[:, j, k * P:(k + 1) * P],
                                              qT[:, j, k * P:(k + 1) * P], start=True, stop=True)
                    mm.then_inc(s_done, 1)

            def head_steps(n, j):
                pe.wait_ge(v_loaded[j], ONE + (n - j) * 8 + 16)
                pe.wait_ge(sf_ready, ONE + 2 * n + 2)
                pe.wait_ge(kw_ready, ONE + n + 1)
                for i in range(STEPS):
                    chunks = ((0, i), (1, C - 1 - i))
                    pe.wait_ge(nd_ready, ONE + (n * STEPS + i - 1 if i else n * STEPS))
                    for d, c in chunks:
                        mm = nc.tensor.matmul(pA[:, i % 2, d * V1:(d + 1) * V1], E[:, j, d, c * P:(c + 1) * P], v1[:, j, c, :], start=True, stop=True)
                    mm.then_inc(a_done, 1)
                    if i < STEPS - 1:
                        pe.wait_ge(cst_ready, ONE + (n * (STEPS - 1) + i - 1 if i else n * (STEPS - 1)))
                        for d, c in chunks:
                            mm = nc.tensor.matmul(pC[:, (i + 1) % 2, d * V1:(d + 1) * V1], kw[:, d, c, :], v1[:, j, c, :], start=True, stop=True)
                        mm.then_inc(c_done, 1)
                    if i:
                        if i == 1:
                            pe.wait_ge(out_ready, ONE + n)
                        if i >= 3:
                            pe.wait_ge(inter_ready, ONE + n * (STEPS - 1) + i - 2)
                        pe.wait_ge(cst_ready, ONE + n * (STEPS - 1) + i)
                        for d, c in chunks:
                            mm = nc.tensor.matmul(pB[:, i % 2, d * V1:(d + 1) * V1], qT[:, j, c * P:(c + 1) * P], cst[:, i % 2, d, :], start=True, stop=True)
                        mm.then_inc(b_done, 1)

            def head_o(n, j):
                pe.wait_ge(hn_ready, ONE + n + 1)
                pe.wait_ge(inter_ready, ONE + (n + 1) * (STEPS - 1))
                for half in range(2):
                    for c in range(C // 2):
                        k = half * (C // 2) + c
                        mm = nc.tensor.transpose(pB[:, half, c * P:(c + 1) * P], hn[:, j, k, :], ident[:, :])
                    mm.then_inc(o_turned, 1)

            head_k(0, 0)
            head_s(0, 0)

            def body(n, j, last):
                if not last:
                    pe.wait_ge(sf_ready, ONE + 2 * n + 2)
                    head_k(n + 1, 1 - j)
                head_steps(n, j)
                if not last:
                    head_s(n + 1, 1 - j)
                head_o(n, j)

            over_heads(pe, body)


ROWS = SEQ // GRID_W
KH, KW = 8, 16
QR, QC = 4, 32
KC_COLS = 40
RB = ROWS // QR
CH = GRID_W // QC
COL0 = [0, GRID_W - KC_COLS]
START = [0, 0, 4, 8]
NROWS = [8, 11, 11, 8]
CHUNK = 3 * KC_COLS
NCH = [3, 4, 4, 3]
WIN = [n * KC_COLS for n in NROWS]
WIN_AT = [sum(WIN[:i]) for i in range(RB)]
CH_AT = [sum(NCH[:i]) for i in range(RB)]
WIN_ALL = sum(WIN)
CH_ALL = sum(NCH)


def attention(nc, io):
    PAIRS = GROUPS * A_HEADS // 2
    U = RB * CH * 2
    RS, RP, RT, RO = 4, 4, 2, 2
    Q_SCALE = float(A_DIM) ** -0.5
    qk = io["qk_t"].rearrange("u (n p) t -> u n p t", p=P)
    v_view = io["vov"].rearrange("u n (r c) d -> u n r c d", c=GRID_W)
    mix = io["mix_t"]
    units = [(ch, rb, hh) for ch in range(CH) for rb in range(RB) for hh in range(2)]
    with ExitStack() as ctx:
        s = Space(nc, ctx, "na")
        ident = s.sb("ident", [P, P])
        qf = s.sb("qf", [P, SEQ])
        kf = s.sb("kf", [P, SEQ])
        q_hi = s.sb("q_hi", [P, 2, SEQ], F32R)
        q_lo = s.sb("q_lo", [P, 2, SEQ], F32R)
        k_hi = s.sb("k_hi", [P, 2, SEQ], F32R)
        k_lo = s.sb("k_lo", [P, 2, SEQ], F32R)
        bias = s.sb("bias", [P, 2, 2, CH, WIN_ALL])
        v = s.sb("v", [P, 2, CH, CH_ALL, P])
        sc = s.sb("sc", [P, RS, max(WIN)])
        pr = s.sb("pr", [P, RP, max(WIN)])
        pt = s.sb("pt", [P, RT, HALF])
        nmax = s.sb("nmax", [P, U])
        sums = s.sb("sums", [P, U])
        gate = s.sb("gate", [P, U])
        rsum = s.sb("rsum", [P, U])
        outT = s.sb("outT", [P, 2, ROWS, GRID_W])
        pS = s.ps("pS", [P, RS, HALF])
        pT = s.ps("pT", [P, RT, HALF])
        pO = s.ps("pO", [P, RO, HALF])

        ready = s.sem("ready")
        q_loaded = s.sem("q_loaded")
        k_loaded = s.sem("k_loaded")
        b_loaded = s.sems("b_loaded", 2)
        v_loaded = s.sems("v_loaded", 2)
        hi_ready = s.sem("hi_ready")
        lo_ready = s.sem("lo_ready")
        qk_done = s.sem("qk_done")
        sc_ready = s.sem("sc_ready")
        exp_ready = s.sem("exp_ready")
        pr_ready = s.sem("pr_ready")
        p_turned = s.sem("p_turned")
        pt_ready = s.sem("pt_ready")
        pv_done = s.sem("pv_done")
        out_ready = s.sem("out_ready")
        out_stored = s.sems("out_stored", 2)
        s.start()
        block = ctx.enter_context(nc.Block())
        V_DMAS = CH * CH_ALL

        def over_pairs(eng, body):
            body(0, 0, True, False)
            with eng.Fori(0, (PAIRS - 2) // 2) as i:
                for j in range(2):
                    body(i * 2 + j + 1, 1 - j, False, False)
            body(PAIRS - 1, 1, False, True)

        def lagged(m, j, i, lag, first):
            if i >= lag:
                return m, j, i - lag
            return None if first else (m - 1, 1 - j, U + i - lag)

        @block.sync
        def _(sp):
            sp.wait_ge(ready, ONE + 1)

            def load(m, hp, j, k):
                sp.wait_ge(lo_ready, ONE + 2 * m)
                sp.dma_start(qf[:, :], qk[2, m]).then_inc(q_loaded, 16)
                sp.dma_start(kf[:, :], qk[3, m]).then_inc(k_loaded, 16)
                if k is not None:
                    sp.wait_ge(pv_done, ONE + (m - 1) * U)
                sp.dma_start(bias[:, j, :, :, :], io["na_bias"][hp]).then_inc(b_loaded[j], 16)
                for ch in range(CH):
                    cols = slice(COL0[ch], COL0[ch] + KC_COLS)
                    for rb in range(RB):
                        for c in range(NCH[rb]):
                            last = c == NCH[rb] - 1
                            p0 = KC_COLS if last else 0
                            r0 = START[rb] + (NROWS[rb] - 2 if last else 3 * c)
                            n = 2 if last else 3
                            sp.dma_start(v[p0:CHUNK, j, ch, CH_AT[rb] + c, :],
                                         v_view[2, m, r0:r0 + n, cols, :]).then_inc(v_loaded[j], 16)

            load(0, 0, 0, None)
            load(1, 1, 1, None)

            def store(m, j):
                sp.wait_ge(out_ready, ONE + (m + 1) * (U // 2))
                sp.dma_start(mix[1, m].rearrange("p (r c) -> p r c", c=GRID_W), outT[:, j, :, :]).then_inc(out_stored[j], 16)

            for hp in range(2):
                load(2 + hp, 2 + hp, hp, 1)
                store(hp, hp)
            with sp.Fori(0, 2) as i:
                for j in range(2):
                    load(i * 2 + j + 4, i * 2 + j, j, 1)
                    store(i * 2 + j + 2, j)
            for j in range(2):
                store(PAIRS - 2 + j, j)
            for j in range(2):
                sp.wait_ge(out_stored[j], ONE + 16 * PAIRS // 2)

        @block.gpsimd
        def _(pool):
            nc.gpsimd.memset(v[0:KC_COLS, :, :, :, :], 0.0)
            identity(nc, pool, ident)
            pool.drain()
            nc.gpsimd.memset(sums[:, :], 0.0).then_inc(ready, 1)

        @block.scalar
        def _(act):
            def split_q(m, j):
                act.wait_ge(q_loaded, ONE + 16 * m + 16)
                nc.scalar.activation(q_hi[:, j, :].rearrange("p (h r c) -> p h r c", h=CH, c=QC),
                                     qf[:, :].rearrange("p (r h c) -> p h r c", h=CH, c=QC), ACT.Copy, scale=Q_SCALE).then_inc(hi_ready, 1)

            def split_k(m, j):
                act.wait_ge(k_loaded, ONE + 16 * m + 16)
                nc.scalar.activation(k_hi[:, j, :], kf[:, :], ACT.Copy).then_inc(hi_ready, 1)

            def body(m, j, first, last):
                for i in range(U):
                    ch, rb, hh = units[i]
                    n = WIN[rb]
                    act.wait_ge(sc_ready, ONE + m * U + i + 1)
                    if not (first and i < RP):
                        act.wait_ge(p_turned, ONE + m * U + i - RP + 1)
                    nc.scalar.activation(pr[:, i % RP, 0:n], sc[:, i % RS, 0:n], ACT.Exp, scale=-1.0, bias=nmax[:, i:i + 1],
                                         accum_out=sums[:, i:i + 1]).then_inc(exp_ready, 1)
                    turn_out(lagged(m, j, i, 2, first), i % RT)
                    give_out(lagged(m, j, i, 3, first))
                    if not last and i == 4:
                        split_q(m + 1, 1 - j)
                    if not last and i == 8:
                        split_k(m + 1, 1 - j)

            def turn_out(at, ring):
                if at is None:
                    return
                m, j, i = at
                w = NCH[units[i][1]] * P
                act.wait_ge(p_turned, ONE + m * U + i + 1)
                act.wait_ge(pv_done, ONE + (m * U + i - RT + 1 if not isinstance(m, int) or m * U + i >= RT else 0))
                nc.scalar.activation(pt[0:CHUNK, i % RT, 0:w], pT[0:CHUNK, i % RT, 0:w], ACT.Copy).then_inc(pt_ready, 1)

            def give_out(at):
                if at is None or units[at[2]][2] == 0:
                    return
                m, j, i = at
                ch, rb, _ = units[i]
                act.wait_ge(pv_done, ONE + m * U + i + 1)
                if i == 1 and not isinstance(m, int) or isinstance(m, int) and m >= 2 and i == 1:
                    act.wait_ge(out_stored[j], ONE + (m - j) * 8)
                nc.scalar.activation(outT[:, j, rb * QR:(rb + 1) * QR, ch * QC:(ch + 1) * QC],
                                     pO[:, (i // 2) % RO, 0:P].rearrange("p (r c) -> p r c", c=QC), ACT.Copy).then_inc(out_ready, 1)

            split_q(0, 0)
            split_k(0, 0)
            over_pairs(act, body)
            for i in range(U, U + 3):
                if i - 2 < U:
                    turn_out((PAIRS - 1, 1, i - 2), None)
                give_out((PAIRS - 1, 1, i - 3))

        @block.vector
        def _(dve):
            def split(m, j, which):
                dve.wait_ge(hi_ready, ONE + 2 * m + 1 + which)
                if which:
                    nc.vector.tensor_tensor(k_lo[:, j, :], kf[:, :], k_hi[:, j, :].bitcast(F32), ALU.subtract).then_inc(lo_ready, 1)
                    return
                for ch in range(CH):
                    tiles = lambda t: t[:, j, ch * HALF:(ch + 1) * HALF].rearrange("p (r c) -> p r c", c=QC)
                    a = nc.vector.scalar_tensor_tensor(tiles(q_lo), qf[:, :].rearrange("p (r h c) -> p h r c", h=CH, c=QC)[:, ch], Q_SCALE,
                                                       tiles(q_hi).bitcast(F32), ALU.mult, ALU.subtract)
                a.then_inc(lo_ready, 1)

            def body(m, j, first, last):
                dve.wait_ge(b_loaded[j], ONE + (m - j) * 8 + 16)
                for i in range(U):
                    ch, rb, hh = units[i]
                    n = WIN[rb]
                    dve.wait_ge(qk_done, ONE + m * U + i + 1)
                    if not (first and i < RS):
                        dve.wait_ge(exp_ready, ONE + m * U + i - RS + 1)
                    nc.vector.memset(gate[:, i:i + 1], 0.0)
                    nc.vector.tensor_tensor_reduce(out=sc[:, i % RS, 0:n], in0=pS[:, i % RS, 0:n],
                                                   in1=bias[:, j, hh, ch, WIN_AT[rb]:WIN_AT[rb] + n], scale=-1.0, scalar=3e38,
                                                   op0=ALU.add, op1=ALU.min, accum_out=nmax[:, i:i + 1]).then_inc(sc_ready, 1)
                    normalise(lagged(m, j, i, 1, first))
                    if not last and i == 4:
                        split(m + 1, 1 - j, 0)
                    if not last and i == 8:
                        split(m + 1, 1 - j, 1)

            def normalise(at):
                if at is None:
                    return
                m, j, i = at
                n = WIN[units[i][1]]
                dve.wait_ge(exp_ready, ONE + m * U + i + 1)
                nc.vector.reciprocal(rsum[:, i:i + 1], sums[:, i:i + 1])
                dve.drain()
                nc.vector.tensor_scalar(pr[:, i % RP, 0:n], pr[:, i % RP, 0:n], rsum[:, i:i + 1], None, ALU.mult).then_inc(pr_ready, 1)

            for which in range(2):
                split(0, 0, which)
            over_pairs(dve, body)
            normalise((PAIRS - 1, 1, U - 1))

        @block.tensor
        def _(pe):
            grid = lambda t, j, hh: t[hh * A_DIM:(hh + 1) * A_DIM, j, :].rearrange("p (r c) -> p r c", c=GRID_W)

            def body(m, j, first, last):
                for i in range(U):
                    ch, rb, hh = units[i]
                    n = WIN[rb]
                    pe.wait_ge(lo_ready, ONE + 2 * m + 2)
                    if not (first and i < RS):
                        pe.wait_ge(sc_ready, ONE + m * U + i - RS + 1)
                    out = pS[:, i % RS, 0:n]
                    for t, (q, k) in enumerate(((q_hi, k_hi), (q_hi, k_lo), (q_lo, k_hi))):
                        tile = (ch * RB + rb) * P
                        mm = nc.tensor.matmul(out, q[hh * A_DIM:(hh + 1) * A_DIM, j, tile:tile + P],
                                              grid(k, j, hh)[:, START[rb]:START[rb] + NROWS[rb], COL0[ch]:COL0[ch] + KC_COLS],
                                              start=(t == 0), stop=(t == 2))
                    mm.then_inc(qk_done, 1)
                    turn(lagged(m, j, i, 2, first))
                    product(lagged(m, j, i, 3, first))

            def turn(at):
                if at is None:
                    return
                m, j, i = at
                rb = units[i][1]
                pe.wait_ge(pr_ready, ONE + m * U + i + 1)
                if not (isinstance(m, int) and m == 0 and i < RT):
                    pe.wait_ge(pt_ready, ONE + m * U + i - RT + 1)
                for c in range(NCH[rb]):
                    k0 = WIN[rb] - CHUNK if c == NCH[rb] - 1 else c * CHUNK
                    mm = nc.tensor.transpose(pT[0:CHUNK, i % RT, c * P:(c + 1) * P], pr[:, i % RP, k0:k0 + CHUNK], ident[:, :])
                mm.then_inc(p_turned, 1)

            def product(at):
                if at is None:
                    return
                m, j, i = at
                ch, rb, hh = units[i]
                pe.wait_ge(pt_ready, ONE + m * U + i + 1)
                if i == 0:
                    pe.wait_ge(v_loaded[j], ONE + (m - j) * 8 * V_DMAS + 16 * V_DMAS)
                if hh == 0 and not (isinstance(m, int) and m == 0 and i // 2 < RO):
                    pe.wait_ge(out_ready, ONE + m * (U // 2) + i // 2 - RO + 1)
                for c in range(NCH[rb]):
                    mm = nc.tensor.matmul(pO[hh * A_DIM:(hh + 1) * A_DIM, (i // 2) % RO, 0:P],
                                          v[0:CHUNK, j, ch, CH_AT[rb] + c, hh * A_DIM:(hh + 1) * A_DIM],
                                          pt[0:CHUNK, i % RT, c * P:(c + 1) * P], start=(c == 0), stop=(c == NCH[rb] - 1))
                mm.then_inc(pv_done, 1)

            pe.wait_ge(ready, ONE + 1)
            over_pairs(pe, body)
            for i in range(U, U + 3):
                if i - 2 < U:
                    turn((PAIRS - 1, 1, i - 2))
                product((PAIRS - 1, 1, i - 3))


def output(nc, io):
    TOK = 2 * P
    NB = SEQ // TOK
    BLOCKS = GROUPS * NB
    x_view = io["x"].rearrange("(t p) n -> t p n", p=P)
    x1_view = io["x1"].rearrange("(t p) n -> t p n", p=P)
    h2_view = io["h2"].rearrange("(t p) n -> t p n", p=P)
    aff_view = io["aff"].rearrange("g e (t p) -> g t e p", p=P)
    mix = io["mix_t"].rearrange("s (g c) p t -> g s p c t", g=GROUPS)
    mod_row = io["mod"].rearrange("g (m n) -> g m n", n=D)
    w_view = io["w_out"].rearrange("(k p) n -> p k n", p=P)
    with ExitStack() as ctx:
        s = Space(nc, ctx, "out", words=5 * P)
        ident = s.part([P, P])
        mhalf = s.part([P, 1])
        base_e = s.part([P, N_EXPERTS])
        gains = s.sb("gains", [P, 2, D])
        rows = s.sb("rows", [P, 2, 3, D])
        w_router = s.part([P, KC, N_EXPERTS])
        wf = s.sb("wf", [P, 2, D])
        w_hi = s.sb("w_hi", [P, KC, D], F32R)
        w_lo = s.sb("w_lo", [P, KC, D], F32R)
        mf = s.sb("mf", [P, 2, KC, TOK])
        m_hi = s.sb("m_hi", [P, 2, KC, TOK], F32R)
        m_lo = s.sb("m_lo", [P, 2, KC, TOK], F32R)
        x = s.sb("x", [P, 2, D])
        h2 = s.sb("h2", [P, 2, D])
        junk = s.sb("junk", [P, D])
        h2T = s.sb("h2T", [P, KC, P])
        ss = s.part([P, 2])
        r = s.part([P, 2])
        logit = s.part([P, N_EXPERTS])
        lmax = s.part([P, 1])
        prob = s.part([P, N_EXPERTS])
        psum = s.part([P, 1])
        aff = s.part([P, N_EXPERTS])
        affT = s.part([N_EXPERTS, 2, P])
        py = s.ps("py", [P, 2, 2, HALF])
        pt = s.ps("pt", [P, 2, HALF])
        pl = s.ps("pl", [P, HALF])
        pa = s.ps("pa", [N_EXPERTS, HALF])

        ready = s.sem("ready")
        c_loaded = s.sem("c_loaded")
        w_loaded = s.sems("w_loaded", 2)
        w_hi_ready = s.sem("w_hi_ready")
        w_lo_ready = s.sem("w_lo_ready")
        rows_loaded = s.sems("rows_loaded", 2)
        rows_ready = s.sem("rows_ready")
        m_loaded = s.sems("m_loaded", 2)
        m_hi_ready = s.sem("m_hi_ready")
        m_lo_ready = s.sem("m_lo_ready")
        x_loaded = s.sems("x_loaded", 2)
        y_done = s.sem("y_done")
        sq_ready = s.sem("sq_ready")
        mean_ready = s.sem("mean_ready")
        r_ready = s.sem("r_ready")
        x1_ready = s.sem("x1_ready")
        x1_stored = s.sems("x1_stored", 2)
        h2_ready = s.sem("h2_ready")
        h2_stored = s.sems("h2_stored", 2)
        h_turned = s.sem("h_turned")
        hT_ready = s.sem("hT_ready")
        l_done = s.sem("l_done")
        l_ready = s.sem("l_ready")
        e_ready = s.sem("e_ready")
        aff_ready = s.sem("aff_ready")
        a_turned = s.sem("a_turned")
        aT_ready = s.sem("aT_ready")
        a_stored = s.sems("a_stored", 2)
        block = ctx.enter_context(nc.Block())

        def over_blocks(eng, body):
            for b in range(4):
                body(b, b % 2, b // 2, b == 0, False)
            for b in range(4, BLOCKS):
                body(b, b % 2, (b // 2) % 2, False, b == BLOCKS - 1)

        @block.sync
        def _(sp):
            def load_mix(b, j):
                if b >= 2:
                    sp.wait_ge(m_lo_ready, b - 1)
                for h in range(2):
                    sp.dma_start(mf[:, j, h * 4:h * 4 + 4, :],
                                 mix[b // NB, h, :, :, b % NB * TOK:b % NB * TOK + TOK]).then_inc(m_loaded[j], 16)

            load_mix(0, 0)
            for k in range(KC):
                if k >= 2:
                    sp.wait_ge(w_lo_ready, k - 1)
                sp.dma_start(wf[:, k % 2, :], w_view[:, k, :]).then_inc(w_loaded[k % 2], 16)
                if k == 1:
                    load_mix(1, 1)
            for i, name in enumerate(("g_post_mix", "g_pre_ffn")):
                sp.dma_start(gains[:, i, :], io[name].to_broadcast([P, D])).then_inc(c_loaded, 16)
            sp.dma_start(w_router[:, :, :], io["w_router"].rearrange("(k p) e -> p k e", p=P)).then_inc(c_loaded, 16)

            def body(b, jb, jr, first, last):
                if b % 2 == 0:
                    if b >= 4:
                        sp.wait_ge(h2_ready, (b - 2) * 2)
                    for i, m in enumerate((GATE1, SCALE2, SHIFT2)):
                        sp.dma_start(rows[:, jr, i, :], mod_row[b // NB, m:m + 1, :].to_broadcast([P, D])).then_inc(rows_loaded[jr], 16)
                for j in range(2):
                    t = b * 2 + j
                    if b:
                        sp.wait_ge(h2_ready, t - 1)
                        sp.wait_ge(x1_stored[j], 16 * b)
                    sp.dma_start(x[:, j, :], x_view[t]).then_inc(x_loaded[j], 16)
                if b + 2 < BLOCKS:
                    load_mix(b + 2, jb)

            over_blocks(sp, body)

        @block.gpsimd
        def _(pool):
            nc.gpsimd.memset(mhalf[:, :], -0.5)
            nc.gpsimd.memset(base_e[:, :], float(np.e))
            identity(nc, pool, ident)
            pool.drain()
            nc.gpsimd.memset(aff[:, :], 0.0).then_inc(ready, 1)
            pool.drain()

            def root(n, j):
                pool.wait_ge(mean_ready, n + 1)
                nc.gpsimd.tensor_tensor(r[:, j:j + 1], ss[:, j:j + 1], mhalf[:, :], ALU.pow).then_inc(r_ready, 1)

            def body(b, jb, jr, first, last):
                for j in range(2):
                    t = b * 2 + j
                    root(2 * t, 0)
                    pool.wait_ge(x1_ready, t + 1)
                    pool.dma_start(x1_view[t], x[:, j, :]).then_inc(x1_stored[j], 16)
                    root(2 * t + 1, 1)
                    pool.wait_ge(h2_ready, t + 1)
                    pool.dma_start(h2_view[t], h2[:, j, :]).then_inc(h2_stored[j], 16)
                    exp_and_store(t - 1, 1 - j)

            def exp_and_store(t, j):
                if t < 0:
                    return
                pool.wait_ge(l_ready, t + 1)
                nc.gpsimd.tensor_tensor(prob[:, :], base_e[:, :], logit[:, :], ALU.pow).then_inc(e_ready, 1)
                if t >= 1:
                    store_aff(t - 1, 1 - j)

            def store_aff(t, j):
                pool.wait_ge(aT_ready, t + 1)
                pool.dma_start(aff_view[t // TT, t % TT], affT[:, j, :]).then_inc(a_stored[j], 16)

            over_blocks(pool, body)
            last = GROUPS * TT - 1
            exp_and_store(last, 1)
            store_aff(last, 1)
            for j in range(2):
                for stored in (x1_stored, h2_stored, a_stored):
                    pool.wait_ge(stored[j], 16 * BLOCKS)

        @block.scalar
        def _(act):
            def split_m(b, j):
                act.wait_ge(m_loaded[j], (b - j) * 16 + 32)
                if b >= 2:
                    act.wait_ge(y_done, (b - 1) * 4)
                nc.scalar.activation(m_hi[:, j, :, :], mf[:, j, :, :], ACT.Copy).then_inc(m_hi_ready, 1)

            split_m(0, 0)
            for k in range(KC):
                act.wait_ge(w_loaded[k % 2], (k // 2) * 16 + 16)
                nc.scalar.activation(w_hi[:, k, :], wf[:, k % 2, :], ACT.Copy).then_inc(w_hi_ready, 1)

            def body(b, jb, jr, first, last):
                if not last:
                    split_m(b + 1, 1 - jb)
                for j in range(2):
                    t = b * 2 + j
                    act.wait_ge(y_done, 2 * t + 2)
                    act.drain()
                    if not (first and j == 0):
                        act.wait_ge(x1_ready, t)
                    nc.scalar.activation(junk[:, :], py[:, j, :, :].rearrange("p a n -> p (a n)"), ACT.Square,
                                         accum_out=ss[:, 0:1]).then_inc(sq_ready, 1)
                    after(t - 1, 1 - j)
                    act.wait_ge(x1_ready, t + 1)
                    nc.scalar.activation(junk[:, :], x[:, j, :], ACT.Square, accum_out=ss[:, 1:2]).then_inc(sq_ready, 1)

            def after(t, j):
                if t < 0:
                    return
                for h in range(2):
                    act.wait_ge(h_turned, 2 * t + h + 1)
                    if t:
                        act.wait_ge(l_done, t)
                    nc.scalar.activation(h2T[:, h * 4:h * 4 + 4, :], pt[:, h, :].rearrange("p (k t) -> p k t", t=P), ACT.Copy).then_inc(hT_ready, 1)
                turn_back(t - 1, 1 - j)

            def turn_back(t, j):
                if t < 0:
                    return
                act.wait_ge(a_turned, t + 1)
                if t >= 2:
                    act.wait_ge(a_stored[j], (t // 2) * 16)
                nc.scalar.activation(affT[:, j, :], pa[:, 0:P], ACT.Copy).then_inc(aT_ready, 1)

            over_blocks(act, body)
            last = GROUPS * TT - 1
            after(last, 1)
            turn_back(last, 1)

        @block.vector
        def _(dve):
            def split_m(b, j):
                dve.wait_ge(m_hi_ready, b + 1)
                nc.vector.tensor_tensor(m_lo[:, j, :, :], mf[:, j, :, :], m_hi[:, j, :, :].bitcast(F32), ALU.subtract).then_inc(m_lo_ready, 1)

            split_m(0, 0)
            for k in range(KC):
                dve.wait_ge(w_hi_ready, k + 1)
                nc.vector.tensor_tensor(w_lo[:, k, :], wf[:, k % 2, :], w_hi[:, k, :].bitcast(F32), ALU.subtract).then_inc(w_lo_ready, 1)
            dve.wait_ge(c_loaded, 48)

            def mean(n, j):
                dve.wait_ge(sq_ready, n + 1)
                nc.vector.tensor_scalar(ss[:, j:j + 1], ss[:, j:j + 1], 1.0 / D, EPS, ALU.mult, ALU.add).then_inc(mean_ready, 1)

            def body(b, jb, jr, first, last):
                if b % 2 == 0:
                    dve.wait_ge(rows_loaded[jr], 48 * (b // 4 + 1))
                    nc.vector.tensor_tensor(rows[:, jr, 0, :], rows[:, jr, 0, :], gains[:, 0, :], ALU.mult)
                    nc.vector.scalar_tensor_tensor(rows[:, jr, 1, :], rows[:, jr, 1, :], 1.0, gains[:, 1, :], ALU.add, ALU.mult)
                    dve.drain()
                if not last:
                    split_m(b + 1, 1 - jb)
                for j in range(2):
                    t = b * 2 + j
                    mean(2 * t, 0)
                    dve.wait_ge(r_ready, 2 * t + 1)
                    y = py[:, j, :, :].rearrange("p a n -> p (a n)")
                    nc.vector.scalar_tensor_tensor(junk[:, :], y, r[:, 0:1], rows[:, jr, 0, :], ALU.mult, ALU.mult)
                    dve.drain()
                    dve.wait_ge(x_loaded[j], 16 * b + 16)
                    nc.vector.tensor_tensor(x[:, j, :], x[:, j, :], junk[:, :], ALU.add).then_inc(x1_ready, 1)
                    softmax_max(t - 1)
                    mean(2 * t + 1, 1)
                    dve.wait_ge(r_ready, 2 * t + 2)
                    if b:
                        dve.wait_ge(h2_stored[j], 16 * b)
                        dve.wait_ge(h_turned, 2 * t - 2)
                    nc.vector.scalar_tensor_tensor(h2[:, j, :], x[:, j, :], r[:, 1:2], rows[:, jr, 1, :], ALU.mult, ALU.mult)
                    dve.drain()
                    nc.vector.tensor_tensor(h2[:, j, :], h2[:, j, :], rows[:, jr, 2, :], ALU.add).then_inc(h2_ready, 1)
                    softmax_rest(t - 1)

            def softmax_max(t):
                if t < 0:
                    return
                dve.wait_ge(l_done, t + 1)
                nc.vector.tensor_reduce(lmax[:, :], pl[:, 0:N_EXPERTS], AX.X, ALU.max)
                dve.drain()
                nc.vector.tensor_scalar(logit[:, :], pl[:, 0:N_EXPERTS], lmax[:, :], None, ALU.subtract).then_inc(l_ready, 1)

            def softmax_rest(t):
                if t < 0:
                    return
                dve.wait_ge(e_ready, t + 1)
                nc.vector.tensor_reduce(psum[:, :], prob[:, :], AX.X, ALU.add)
                dve.drain()
                nc.vector.reciprocal(psum[:, :], psum[:, :])
                dve.drain()
                if t:
                    dve.wait_ge(a_turned, t)
                nc.vector.tensor_scalar(aff[:, :], prob[:, :], psum[:, :], None, ALU.mult).then_inc(aff_ready, 1)

            over_blocks(dve, body)
            softmax_max(GROUPS * TT - 1)
            softmax_rest(GROUPS * TT - 1)

        @block.tensor
        def _(pe):
            pe.wait_ge(ready, 1)

            def y_half(t, j, jb, half):
                pe.wait_ge(m_lo_ready, t // 2 + 1)
                if t >= 2:
                    pe.wait_ge(x1_ready, t - 1)
                for k in range(KC):
                    if t == 0 and half == 0:
                        pe.wait_ge(w_lo_ready, k + 1)
                    for i, (m, w) in enumerate(((m_hi, w_hi), (m_hi, w_lo), (m_lo, w_hi))):
                        mm = nc.tensor.matmul(py[:, j, half, :], m[:, jb, k, j * P:(j + 1) * P], w[:, k, half * HALF:(half + 1) * HALF],
                                              start=(k == 0 and i == 0), stop=(k == KC - 1 and i == 2))
                mm.then_inc(y_done, 1)

            def turn(t, j):
                if t < 0:
                    return
                pe.wait_ge(h2_ready, t + 1)
                for h in range(2):
                    if t:
                        pe.wait_ge(hT_ready, 2 * t + h - 1)
                    for k in range(4):
                        c = h * 4 + k
                        mm = nc.tensor.transpose(pt[:, h, k * P:(k + 1) * P], h2[:, j, c * P:(c + 1) * P], ident[:, :])
                    mm.then_inc(h_turned, 1)

            def route(t):
                if t < 0:
                    return
                pe.wait_ge(hT_ready, 2 * t + 2)
                if t:
                    pe.wait_ge(l_ready, t)
                for k in range(KC):
                    mm = nc.tensor.matmul(pl[:, 0:N_EXPERTS], h2T[:, k, :], w_router[:, k, :], start=(k == 0), stop=(k == KC - 1))
                mm.then_inc(l_done, 1)

            def turn_aff(t):
                if t < 0:
                    return
                pe.wait_ge(aff_ready, t + 1)
                if t:
                    pe.wait_ge(aT_ready, t)
                nc.tensor.transpose(pa[:, 0:P], aff[:, :], ident[:, :]).then_inc(a_turned, 1)

            def body(b, jb, jr, first, last):
                for j in range(2):
                    t = b * 2 + j
                    y_half(t, j, jb, 0)
                    turn(t - 1, 1 - j)
                    turn_aff(t - 2)
                    y_half(t, j, jb, 1)
                    if t == 1:
                        pe.wait_ge(c_loaded, 48)
                    route(t - 1)

            over_blocks(pe, body)
            last = GROUPS * TT - 1
            turn(last, 1)
            turn_aff(last - 1)
            route(last)
            turn_aff(last)


def experts(nc, io):
    NE = N_EXPERTS
    R = GROUPS * NE
    ROUNDS = CAP // 8
    PIECE = 2
    NP = KC // PIECE
    GATE, UP, DOWN = range(3)
    ZEROS = GROUPS * TT
    BK = 4
    mats = [io[f"w_expert_{n}"].rearrange("e (q a p) n -> e q p a n", p=P, a=PIECE) for n in ("gate", "up", "down")]
    with ExitStack() as ctx:
        s = Space(nc, ctx, "moe", words=21 * P)
        ident = s.part([P, P])
        aff = s.part([R, SEQ])
        left = s.part([R, SEQ])
        gate = s.part([R, CAP])
        index = s.part([R, CAP], U32)
        index_f = s.part([R, CAP])
        row0 = s.part([R, 1])
        gate_c = s.part([P, R])
        index_c = s.part([P, R], U32)
        zero = s.sb("zero", [P, D])
        idx_in = s.part([P, 2, GROUPS], U32)
        idx_out = s.part([P, 2, GROUPS], U32)
        gcol = s.part([P, 2, GROUPS])
        wf = s.sb("wf", [P, NP, PIECE, D])
        w_hi = s.sb("w_hi", [P, NP, PIECE, D], F32R)
        w_lo = s.sb("w_lo", [P, NP, PIECE, D], F32R)
        xe = s.sb("xe", [P, GROUPS, D])
        x_hi = s.sb("x_hi", [P, 2, GROUPS, KC, P], F32R)
        x_lo = s.sb("x_lo", [P, 2, GROUPS, KC, P], F32R)
        hid = s.sb("hid", [P, GROUPS, D])
        h_hi = s.sb("h_hi", [P, GROUPS, KC, P], F32R)
        h_lo = s.sb("h_lo", [P, GROUPS, KC, P], F32R)
        ye = s.sb("ye", [P, GROUPS, D])
        acc = s.ps("acc", [P, 2, BK, HALF])

        ready = s.sem("ready")
        a_loaded = s.sem("a_loaded")
        top_ready = s.sem("top_ready")
        top_turned = s.sem("top_turned")
        cols_ready = s.sem("cols_ready")
        w_loaded = s.sems("w_loaded", NP)
        w_hi_ready = s.sem("w_hi_ready")
        w_lo_ready = s.sem("w_lo_ready")
        piece_done = s.sem("piece_done")
        gcol_ready = s.sem("gcol_ready")
        gathered = s.soft_sem("gathered")
        x_turned = s.sem("x_turned")
        x_hi_ready = s.sem("x_hi_ready")
        x_ready = s.sem("x_ready")
        silu_ready = s.sem("silu_ready")
        hid_ready = s.sem("hid_ready")
        h_turned = s.sem("h_turned")
        h_hi_ready = s.sem("h_hi_ready")
        h_ready = s.sem("h_ready")
        ye_ready = s.sem("ye_ready")
        added = s.soft_sem("added")
        s.start()
        block = ctx.enter_context(nc.Block())

        def piece(e, step, q):
            if step == GATE:
                at = 0 if isinstance(e, int) and e == 0 else 3 * e - 1
            elif step == UP:
                at = 3 * e + 1
            else:
                at = 3 * e + (2 if isinstance(e, int) and e == NE - 1 else 3)
            return at * NP + q

        def over_experts(eng, body):
            with eng.Fori(0, NE // 2 - 1) as i:
                for j in range(2):
                    body(i * 2 + j, j)
            for j in range(2):
                body(NE - 2 + j, j)

        def is_last(e, n=1):
            return isinstance(e, int) and e >= NE - n

        @block.sync
        def _(sp):
            sp.dma_start(aff[:, :], io["aff"].rearrange("g e t -> (g e) t")).then_inc(a_loaded, 16)

            def load(e, step, first=False):
                for q in range(NP):
                    if not first:
                        sp.wait_ge(w_lo_ready, ONE + piece(e, step, q) - NP + 1)
                    sp.dma_start(wf[:, q, :, :], mats[step][e, q]).then_inc(w_loaded[q], 16)

            load(0, GATE, True)

            def body(e, j):
                load(e, UP)
                if not is_last(e):
                    load(e + 1, GATE)
                load(e, DOWN)

            over_experts(sp, body)

        @block.gpsimd
        def _(pool):
            nc.gpsimd.memset(zero[:, :], 0.0)
            nc.gpsimd.memset(row0[:, :], float(SEQ))
            identity(nc, pool, ident)
            pool.drain()
            nc.gpsimd.affine_select(out=row0[:, :], in_=row0[:, :], compare_op=ALU.is_ge, fill=0.0, base=-NE,
                                    pattern=[[0, 1]], channel_multiplier=1).then_inc(ready, 1)
            for t in range(ZEROS):
                pool.dma_start(io["y"][t * P:(t + 1) * P, :], zero[:, :]).then_inc(added, 16)
            pool.wait_ge(cols_ready, ONE + 2)
            by_expert = lambda t, e: t[:, :].rearrange("p (g e) -> p g e", g=GROUPS)[:, :, bass.ds(e, 1)].squeeze(2)

            def gather(e, j, first=False):
                if not first:
                    pool.wait_ge(x_turned, ONE + e * BK)
                nc.gpsimd.tensor_copy(idx_in[:, j, :], by_expert(index_c, e))
                pool.drain()
                for g in range(GROUPS):
                    pool.indirect_dma_start(xe[:, g, :], None, io["h2"], bass.IndirectOffsetOnAxis(ap=idx_in[:, j, g:g + 1], axis=0)).then_inc(gathered, 16)

            def scatter(e, j):
                nc.gpsimd.tensor_copy(gcol[:, j, :], by_expert(gate_c, e)).then_inc(gcol_ready, 1)
                for g in range(GROUPS):
                    pool.wait_ge(ye_ready, ONE + e * GROUPS + g + 1)
                    pool.wait_ge(added, (ZEROS + e * GROUPS + g) * 16)
                    nc.gpsimd.tensor_copy(idx_out[:, j, g:g + 1], index_c[:, bass.ds(e + g * NE, 1)])
                    pool.drain()
                    pool.indirect_dma_start(io["y"], bass.IndirectOffsetOnAxis(ap=idx_out[:, j, g:g + 1], axis=0), ye[:, g, :], None,
                                            compute_op=ALU.add).then_inc(added, 16)

            gather(0, 0, True)
            gather(1, 1)

            def body(e, j):
                if not is_last(e, 2):
                    gather(e + 2, j)
                scatter(e, j)

            over_experts(pool, body)
            pool.wait_ge(added, (ZEROS + GROUPS * NE) * 16)

        @block.scalar
        def _(act):
            def split(e, step, qs=range(NP), first=False):
                for q in qs:
                    n = piece(e, step, q)
                    act.wait_ge(w_loaded[q], ONE + piece(e, step, 0) * (16 // NP) + 16)
                    if not first:
                        act.wait_ge(piece_done, ONE + n - NP + 1)
                    nc.scalar.activation(w_hi[:, q, :, :], wf[:, q, :, :], ACT.Copy).then_inc(w_hi_ready, 1)

            def turned_out(e, dst, turned, done):
                for b in range(BK):
                    act.wait_ge(turned, ONE + e * BK + b + 1)
                    bank = acc[:, dst[1], b, :].rearrange("p (k t) -> p k t", t=P)
                    nc.scalar.activation(dst[0][:, b // 2, b % 2 * 4:b % 2 * 4 + 4, :], bank, ACT.Copy).then_inc(done, 1)

            def silu(e, j, first=False):
                act.wait_ge(piece_done, ONE + piece(e, GATE, NP))
                if not first:
                    act.wait_ge(h_turned, ONE + e * BK)
                for b in range(BK):
                    nc.scalar.activation(hid[:, b // 2, b % 2 * HALF:(b % 2 + 1) * HALF], acc[:, j, b, :], ACT.Silu).then_inc(silu_ready, 1)

            def weigh(e, j):
                act.wait_ge(piece_done, ONE + piece(e, DOWN, NP))
                act.wait_ge(gcol_ready, ONE + e + 1)
                act.wait_ge(added, (ZEROS + e * GROUPS) * 16)
                for b in range(BK):
                    a = nc.scalar.activation(ye[:, b // 2, b % 2 * HALF:(b % 2 + 1) * HALF], acc[:, j, b, :], ACT.Copy,
                                             scale=gcol[:, j, b // 2:b // 2 + 1])
                    if b % 2:
                        a.then_inc(ye_ready, 1)

            split(0, GATE, first=True)
            turned_out(0, (x_hi[:, 0], 0), x_turned, x_hi_ready)
            split(0, UP)
            silu(0, 0, True)

            def body(e, j):
                if is_last(e):
                    split(e, DOWN)
                else:
                    split(e + 1, GATE, range(0, 2))
                    turned_out(e + 1, (x_hi[:, 1 - j], 1 - j), x_turned, x_hi_ready)
                    split(e + 1, GATE, range(2, NP))
                    split(e, DOWN, range(0, 2))
                turned_out(e, (h_hi, j), h_turned, h_hi_ready)
                if not is_last(e):
                    split(e, DOWN, range(2, NP))
                    silu(e + 1, 1 - j)
                    split(e + 1, UP)
                weigh(e, j)

            over_experts(act, body)

        @block.vector
        def _(dve):
            dve.wait_ge(a_loaded, ONE + 16)
            src = aff
            for r in range(ROUNDS):
                c = slice(8 * r, 8 * r + 8)
                nc.vector.max(gate[:, c], src[:, :])
                dve.drain()
                nc.vector.max_index(index[:, c], gate[:, c], src[:, :])
                if r < ROUNDS - 1:
                    nc.vector.match_replace(left[:, :], gate[:, c], src[:, :], NEG)
                    src = left
                dve.drain()
            dve.wait_ge(ready, ONE + 1)
            nc.vector.tensor_copy(index_f[:, :], index[:, :])
            dve.drain()
            nc.vector.tensor_scalar(index_f[:, :], index_f[:, :], row0[:, :], None, ALU.add).then_inc(top_ready, 1)
            dve.wait_ge(top_turned, ONE + 1)
            nc.vector.tensor_copy(gate_c[:, :], acc[:, 0, 0, 0:R]).then_inc(cols_ready, 1)
            nc.vector.tensor_copy(index_c[:, :], acc[:, 0, 0, R:2 * R]).then_inc(cols_ready, 1)

            def split(e, step, qs=range(NP)):
                for q in qs:
                    dve.wait_ge(w_hi_ready, ONE + piece(e, step, q) + 1)
                    nc.vector.tensor_tensor(w_lo[:, q, :, :], wf[:, q, :, :], w_hi[:, q, :, :].bitcast(F32), ALU.subtract).then_inc(w_lo_ready, 1)

            def turned_out(e, hi, lo, j, hi_ready, done):
                for b in range(BK):
                    dve.wait_ge(hi_ready, ONE + e * BK + b + 1)
                    part = lambda t: t[:, b // 2, b % 2 * 4:b % 2 * 4 + 4, :].rearrange("p k t -> p (k t)")
                    nc.vector.tensor_tensor(part(lo), acc[:, j, b, :], part(hi).bitcast(F32), ALU.subtract).then_inc(done, 1)

            def multiply(e, j):
                dve.wait_ge(piece_done, ONE + piece(e, UP, NP))
                for b in range(BK):
                    part = hid[:, b // 2, b % 2 * HALF:(b % 2 + 1) * HALF]
                    nc.vector.tensor_tensor(part, part, acc[:, j, b, :], ALU.mult).then_inc(hid_ready, 1)

            split(0, GATE)
            turned_out(0, x_hi[:, 0], x_lo[:, 0], 0, x_hi_ready, x_ready)
            split(0, UP)

            def body(e, j):
                if is_last(e):
                    split(e, DOWN)
                    multiply(e, j)
                else:
                    split(e + 1, GATE, range(0, 2))
                    turned_out(e + 1, x_hi[:, 1 - j], x_lo[:, 1 - j], 1 - j, x_hi_ready, x_ready)
                    split(e + 1, GATE, range(2, NP))
                    multiply(e, j)
                    split(e, DOWN, range(0, 2))
                turned_out(e, h_hi, h_lo, j, h_hi_ready, h_ready)
                if not is_last(e):
                    split(e, DOWN, range(2, NP))
                    split(e + 1, UP)

            over_experts(dve, body)

        @block.tensor
        def _(pe):
            pe.wait_ge(ready, ONE + 1)
            pe.wait_ge(top_ready, ONE + 1)
            nc.tensor.transpose(acc[:, 0, 0, 0:R], gate[:, :], ident[0:R, 0:R])
            nc.tensor.transpose(acc[:, 0, 0, R:2 * R], index_f[:, :], ident[0:R, 0:R]).then_inc(top_turned, 1)
            pe.wait_ge(cols_ready, ONE + 2)

            def products(e, step, j, hi, lo, qs=range(NP)):
                for q in qs:
                    pe.wait_ge(w_lo_ready, ONE + piece(e, step, q) + 1)
                    for b in range(BK):
                        g, h = b // 2, b % 2
                        for a in range(PIECE):
                            k = q * PIECE + a
                            for i, (x, w) in enumerate(((hi, w_hi), (hi, w_lo), (lo, w_hi))):
                                mm = nc.tensor.matmul(acc[:, j, b, :], x[:, g, k, :], w[:, q, a, h * HALF:(h + 1) * HALF],
                                                      start=(k == 0 and i == 0), stop=(k == KC - 1 and i == 2))
                    mm.then_inc(piece_done, 1)

            def turn(rows, j, done):
                for b in range(BK):
                    for k in range(4):
                        c = (b % 2) * 4 + k
                        mm = nc.tensor.transpose(acc[:, j, b, k * P:(k + 1) * P], rows[:, b // 2, c * P:(c + 1) * P], ident[:, :])
                    mm.then_inc(done, 1)

            def turn_x(e, j, first=False):
                pe.wait_ge(gathered, (e + 1) * GROUPS * 16)
                if not first:
                    pe.wait_ge(ye_ready, ONE + (e - 1) * GROUPS)
                turn(xe, j, x_turned)

            def turn_h(e, j):
                pe.wait_ge(hid_ready, ONE + e * BK + BK)
                turn(hid, j, h_turned)

            turn_x(0, 0, True)
            pe.wait_ge(x_ready, ONE + BK)
            products(0, GATE, 0, x_hi[:, 0], x_lo[:, 0])

            def body(e, j):
                first, second = range(0, 2), range(2, NP)
                pe.wait_ge(silu_ready, ONE + e * BK + BK)
                products(e, UP, j, x_hi[:, j], x_lo[:, j], first)
                if not is_last(e):
                    turn_x(e + 1, 1 - j)
                products(e, UP, j, x_hi[:, j], x_lo[:, j], second)
                if not is_last(e):
                    pe.wait_ge(x_ready, ONE + e * BK + 2 * BK)
                    products(e + 1, GATE, 1 - j, x_hi[:, 1 - j], x_lo[:, 1 - j], first)
                turn_h(e, j)
                if not is_last(e):
                    products(e + 1, GATE, 1 - j, x_hi[:, 1 - j], x_lo[:, 1 - j], second)
                pe.wait_ge(h_ready, ONE + e * BK + BK)
                products(e, DOWN, j, h_hi, h_lo)

            over_experts(pe, body)


def finish(nc, io):
    SLOTS = 4
    tiles = lambda t: t.rearrange("(i j p) n -> i j p n", j=SLOTS, p=P)
    y_view, x1_view, out_view = tiles(io["y"]), tiles(io["x1"]), tiles(io["out"])
    N = GROUPS * TT // SLOTS
    mod_row = io["mod"].rearrange("g (m n) -> g m n", n=D)
    with ExitStack() as ctx:
        s = Space(nc, ctx, "fin")
        gain = s.sb("gain", [P, D])
        rows = s.sb("rows", [P, GROUPS, D])
        y = s.sb("y", [P, SLOTS, D])
        x = s.sb("x", [P, SLOTS, D])
        junk = s.sb("junk", [P, 2, D])
        mhalf = s.sb("mhalf", [P, 1])
        ss = s.sb("ss", [P, SLOTS])
        r = s.sb("r", [P, SLOTS])
        c_loaded = s.sem("c_loaded")
        ready = s.sem("ready")
        rows_ready = s.sem("rows_ready")
        y_loaded = s.sems("y_loaded", SLOTS)
        x_loaded = s.sems("x_loaded", SLOTS)
        sq_ready = s.sem("sq_ready")
        mean_ready = s.sem("mean_ready")
        r_ready = s.sem("r_ready")
        scaled = s.sem("scaled")
        out_ready = s.sem("out_ready")
        stored = s.sems("stored", SLOTS)
        block = ctx.enter_context(nc.Block())

        @block.sync
        def _(sp):
            sp.dma_start(gain[:, :], io["g_post_ffn"].to_broadcast([P, D])).then_inc(c_loaded, 16)
            for g in range(GROUPS):
                sp.dma_start(rows[:, g, :], mod_row[g, GATE2:GATE2 + 1, :].to_broadcast([P, D])).then_inc(c_loaded, 16)
            for i in range(N):
                for j in range(SLOTS):
                    if i:
                        sp.wait_ge(out_ready, (i - 1) * SLOTS + j + 1)
                        sp.wait_ge(stored[j], i * 16)
                    sp.dma_start(y[:, j, :], y_view[i, j]).then_inc(y_loaded[j], 16)
                    sp.dma_start(x[:, j, :], x1_view[i, j]).then_inc(x_loaded[j], 16)

        @block.gpsimd
        def _(pool):
            nc.gpsimd.memset(mhalf[:, :], -0.5)
            pool.drain()
            for i in range(N):
                for j in range(SLOTS):
                    pool.wait_ge(mean_ready, i * SLOTS + j + 1)
                    nc.gpsimd.tensor_tensor(r[:, j:j + 1], ss[:, j:j + 1], mhalf[:, :], ALU.pow).then_inc(r_ready, 1)

        @block.scalar
        def _(act):
            def store(i, j):
                act.wait_ge(out_ready, i * SLOTS + j + 1)
                act.dma_start(out_view[i, j], x[:, j, :]).then_inc(stored[j], 16)

            for i in range(N):
                for j in range(SLOTS):
                    act.wait_ge(y_loaded[j], 16 * i + 16)
                    if i:
                        act.wait_ge(r_ready, (i - 1) * SLOTS + j + 1)
                    act.drain()
                    nc.scalar.activation(junk[:, j % 2, :], y[:, j, :], ACT.Square, accum_out=ss[:, j:j + 1]).then_inc(sq_ready, 1)
                    if j >= 2:
                        store(i, j - 2)
                    elif i:
                        store(i - 1, j + 2)
            for j in range(2, SLOTS):
                store(N - 1, j)
            for j in range(SLOTS):
                act.wait_ge(stored[j], 16 * N)

        @block.vector
        def _(dve):
            dve.wait_ge(c_loaded, 16 * (GROUPS + 1))
            for g in range(GROUPS):
                nc.vector.tensor_tensor(rows[:, g, :], rows[:, g, :], gain[:, :], ALU.mult)
            dve.drain()

            def mean(i, j):
                dve.wait_ge(sq_ready, i * SLOTS + j + 1)
                nc.vector.tensor_scalar(ss[:, j:j + 1], ss[:, j:j + 1], 1.0 / D, EPS, ALU.mult, ALU.add).then_inc(mean_ready, 1)

            mean(0, 0)
            for n in range(N * SLOTS):
                i, j = n // SLOTS, n % SLOTS
                if n + 1 < N * SLOTS:
                    mean((n + 1) // SLOTS, (n + 1) % SLOTS)
                dve.wait_ge(r_ready, n + 1)
                nc.vector.scalar_tensor_tensor(y[:, j, :], y[:, j, :], r[:, j:j + 1], rows[:, n // TT, :], ALU.mult, ALU.mult)
                dve.drain()
                dve.wait_ge(x_loaded[j], 16 * i + 16)
                nc.vector.tensor_tensor(x[:, j, :], x[:, j, :], y[:, j, :], ALU.add).then_inc(out_ready, 1)


def layer(nc, io):
    for name, shape in (("mod", [GROUPS, N_MOD * D]), ("qk_t", [4, D, SEQ]), ("vov", [3, KC, SEQ, P]),
                        ("gates_t", [GROUPS, GATES, SEQ]), ("nmx", [40, SEQ]), ("sold", [40, SEQ // P]),
                        ("mix_t", [GROUPS, KC, P, SEQ]), ("x1", [GROUPS * SEQ, D]), ("h2", [GROUPS * SEQ, D]),
                        ("aff", [GROUPS, N_EXPERTS, SEQ]), ("y", [GROUPS * SEQ, D])):
        io[name] = nc.dram_tensor(f"scratch_{name}", shape, F32, kind="Internal").ap()
    adaln(nc, io)
    projections(nc, io)
    mlstm(nc, io)
    attention(nc, io)
    output(nc, io)
    experts(nc, io)
    finish(nc, io)


def na_windows(rel_bias):
    flat = np.concatenate([rel_bias.reshape(-1), np.full(1, NEG, rel_bias.dtype)])
    rows, kh, kw = SEQ // GRID_W, 8, 16
    cols_q, cols_k = 32, 40
    first_row, n_rows = [0, 0, 4, 8], [8, 11, 11, 8]
    q = np.arange(P)
    heads = []
    for head in range(A_HEADS):
        parts = []
        for half in range(2):
            for block in range(4):
                key = np.arange(n_rows[block] * cols_k)
                qr, qc = block * 4 + q[:, None] // cols_q, half * cols_q + q[:, None] % cols_q
                kr, kc = first_row[block] + key[None] // cols_k, (0, 24)[half] + key[None] % cols_k
                r0, c0 = np.clip(qr - kh // 2, 0, rows - kh), np.clip(qc - kw // 2, 0, GRID_W - kw)
                inside = (kr >= r0) & (kr < r0 + kh) & (kc >= c0) & (kc < c0 + kw)
                at = (head * (2 * kh - 1) + kr - qr + kh - 1) * (2 * kw - 1) + kc - qc + kw - 1
                parts.append(np.where(inside, at, flat.size - 1))
        heads.append(np.concatenate(parts, 1))
    at = np.stack(heads).reshape(A_HEADS // 2, 2, P, 2, -1).transpose(0, 2, 1, 3, 4)
    return flat[at]


def kernel(**inputs):
    import concourse.bacc as bacc
    from concourse.bass_utils import run_bass_kernel_spmd

    a = {name: np.asarray(value) for name, value in inputs.items()}
    w_in = a["w_in"][0]
    q_m, k_m, v_m, o_m, gates, q_n, k_n, v_n = np.split(w_in, [MW, 2 * MW, 3 * MW, 4 * MW, 4 * MW + GATES, 5 * MW + GATES, 6 * MW + GATES], axis=1)
    b_gates = np.zeros((40, 2), a["b_gates"].dtype)
    for d in range(2):
        for g in range(GROUPS):
            b_gates[d * 32 + g * M_HEADS:d * 32 + (g + 1) * M_HEADS] = a["b_gates"][0, d].T
    arrays = {
        "x": np.concatenate([a["x_prompt"][0], a["x_sample"][0]]),
        "c_t": np.stack([a["c_prompt"][0], a["c_sample"][0]], -1).reshape(KC, P, GROUPS).transpose(1, 0, 2),
        "w_ada": a["w_ada"][0],
        "b_ada": a["b_ada"],
        "g_pre_mix": a["g_pre_mix"][0].reshape(KC, P).T,
        "w_units": np.stack([q_m, k_m, q_n, k_n, v_m, o_m, v_n]).reshape(7, KC, P, MW).transpose(0, 2, 1, 3),
        "w_gates": gates.reshape(KC, P, GATES).transpose(1, 0, 2),
        "b_gates": b_gates,
        "g_mlstm": np.tile(a["g_mlstm"][0].T, (1, GROUPS)),
        "na_bias": na_windows(a["na_rel_bias"][0]),
        "g_post_mix": a["g_post_mix"],
        "g_pre_ffn": a["g_pre_ffn"],
        "w_out": a["w_out"][0],
        "w_router": a["w_router"][0],
        "g_post_ffn": a["g_post_ffn"],
        "w_expert_gate": a["w_expert_gate"][0],
        "w_expert_up": a["w_expert_up"][0],
        "w_expert_down": a["w_expert_down"][0],
    }
    arrays = {f"in_{name}": np.ascontiguousarray(value) for name, value in arrays.items()}
    nc = bacc.Bacc("TRN2", target_bir_lowering=False, num_devices=1)
    io = {name[3:]: nc.dram_tensor(name, value.shape, mybir.dt.from_np(value.dtype), kind="ExternalInput").ap()
          for name, value in arrays.items()}
    io["out"] = nc.dram_tensor("out", [GROUPS * SEQ, D], F32, kind="ExternalOutput").ap()
    layer(nc, io)
    out = run_bass_kernel_spmd(nc, [arrays], core_ids=[0]).results[0]["out"]
    return out[:SEQ][None], out[SEQ:][None]
```
